# Optimizing a Trainium2 kernel written in Bass

```python
import math
import jax, jax.numpy as jnp
from jax import lax
import numpy as np

D_MODEL = 1024
BATCH = 1
SEQ = 512
DEPTH = 1
DEC_BATCH = 1
DEC_SEQ = 256
PAST_LEN = 128

SSM_EXPAND = 2
D_INNER = SSM_EXPAND * D_MODEL
SSM_HEAD_DIM = 64
SSM_HEADS = D_INNER // SSM_HEAD_DIM
SSM_GROUPS = 8
HEADS_PER_GROUP = SSM_HEADS // SSM_GROUPS
D_STATE = 128
CONV_K = 5
CHUNK = 128
CONV_CH = D_INNER + 2 * SSM_GROUPS * D_STATE
DT_MIN = 1e-3
DT_MAX = 1e-1
POOL_WIDTH = D_MODEL
POOL_WINDOWS = (2, 4, 8, 16)
POOL_GROUPS = len(POOL_WINDOWS)
POOL_GROUP_DIM = POOL_WIDTH // POOL_GROUPS
N_EXPERTS = 16
CAPACITY_FACTOR = 2
EXPERT_FF = 2816
EPS = 1e-6
IN_COLS = D_INNER + CONV_CH + 2 * SSM_HEADS + POOL_WIDTH + 2 * D_MODEL

kernel_name = "hybrid_ssd_pool_ec_encoder"

def rms_norm(x, w):
    xf = x.astype(jnp.float32)
    y = xf * lax.rsqrt(jnp.mean(xf * xf, axis=-1, keepdims=True) + EPS)
    return (y * w.astype(jnp.float32)).astype(x.dtype)

def grouped_rms_norm(y, w):
    b, l, d = y.shape
    yf = y.astype(jnp.float32).reshape(b, l, SSM_GROUPS, d // SSM_GROUPS)
    yf = yf * lax.rsqrt(jnp.mean(yf * yf, axis=-1, keepdims=True) + EPS)
    return (yf.reshape(b, l, d) * w.astype(jnp.float32)).astype(y.dtype)

def centred_dwconv(u, w, b):
    pad = CONV_K // 2
    y = lax.conv_general_dilated(
        u, w[:, None, :].astype(u.dtype), window_strides=(1,), padding=[(pad, pad)],
        dimension_numbers=("NWC", "WIO", "NWC"), feature_group_count=u.shape[-1])
    return y + b.astype(u.dtype)

def ssd_scan(xh, dt, a, bm, cm):
    bsz, seq, _, p = xh.shape
    nc = seq // CHUNK
    g, r, n = SSM_GROUPS, HEADS_PER_GROUP, D_STATE
    xdt = (xh.astype(jnp.float32) * dt[..., None]).reshape(bsz, nc, CHUNK, g, r, p)
    acum = jnp.cumsum((dt * a).reshape(bsz, nc, CHUNK, g, r), axis=2)
    bc = bm.astype(jnp.float32).reshape(bsz, nc, CHUNK, g, n)
    cc = cm.astype(jnp.float32).reshape(bsz, nc, CHUNK, g, n)
    seg = acum[:, :, :, None] - acum[:, :, None, :]
    lower = jnp.tril(jnp.ones((CHUNK, CHUNK), dtype=bool))[:, :, None, None]
    decay = jnp.exp(jnp.where(lower, seg, -jnp.inf))
    cb = jnp.einsum("bclgn,bcsgn->bclsg", cc, bc)
    y_diag = jnp.einsum("bclsgr,bcsgrp->bclgrp", cb[..., None] * decay, xdt)
    d_end = jnp.exp(acum[:, :, -1:] - acum)
    d_chunk = jnp.exp(acum[:, :, -1])
    d_start = jnp.exp(acum)

    def step(state, inp):
        x_c, b_c, c_c, de_c, dc_c, ds_c = inp
        y_off = jnp.einsum("blgn,bgrpn,blgr->blgrp", c_c, state, ds_c)
        new_state = state * dc_c[..., None, None] + jnp.einsum("blgn,blgr,blgrp->bgrpn", b_c, de_c, x_c)
        return new_state, y_off

    xs = (jnp.moveaxis(xdt, 1, 0), jnp.moveaxis(bc, 1, 0), jnp.moveaxis(cc, 1, 0),
          jnp.moveaxis(d_end, 1, 0), jnp.moveaxis(d_chunk, 1, 0), jnp.moveaxis(d_start, 1, 0))
    init = jnp.zeros((bsz, g, r, p, n), jnp.float32)
    _, y_off = lax.scan(step, init, xs)
    y = y_diag + jnp.moveaxis(y_off, 0, 1)
    return y.reshape(bsz, seq, SSM_HEADS, p)

def ssd_branch(z, xbc, dt_f_raw, dt_b_raw, conv_w, conv_b, dt_bias_f, dt_bias_b,
               a_log_f, a_log_b, d_skip, ssm_norm_w, w_ssm_out):
    bsz, seq, _ = z.shape
    xbc = jax.nn.silu(centred_dwconv(xbc, conv_w, conv_b))
    xs, bm, cm = jnp.split(xbc, [D_INNER, D_INNER + SSM_GROUPS * D_STATE], axis=-1)
    xh = xs.reshape(bsz, seq, SSM_HEADS, SSM_HEAD_DIM)
    bm = bm.reshape(bsz, seq, SSM_GROUPS, D_STATE)
    cm = cm.reshape(bsz, seq, SSM_GROUPS, D_STATE)
    dt_f = jax.nn.softplus(dt_f_raw.astype(jnp.float32) + dt_bias_f.astype(jnp.float32))
    dt_b = jax.nn.softplus(dt_b_raw.astype(jnp.float32) + dt_bias_b.astype(jnp.float32))
    a_f = -jnp.exp(a_log_f.astype(jnp.float32))
    a_b = -jnp.exp(a_log_b.astype(jnp.float32))
    y_f = ssd_scan(xh, dt_f, a_f, bm, cm)
    flip = lambda t: jnp.flip(t, axis=1)
    y_b = flip(ssd_scan(flip(xh), flip(dt_b), a_b, flip(bm), flip(cm)))
    y = y_f + y_b + xh.astype(jnp.float32) * d_skip.astype(jnp.float32)[:, None]
    y = y.reshape(bsz, seq, D_INNER).astype(z.dtype)
    y = grouped_rms_norm(y * jax.nn.silu(z), ssm_norm_w)
    return y @ w_ssm_out

def pool_branch(u, w_pool, pool_scale):
    bsz, seq, _ = u.shape
    uf = u.astype(jnp.float32).reshape(bsz, seq, POOL_GROUPS, POOL_GROUP_DIM)
    csum = jnp.concatenate([jnp.zeros((bsz, 1, POOL_GROUPS, POOL_GROUP_DIM), jnp.float32),
                            jnp.cumsum(uf, axis=1)], axis=1)
    pos = jnp.arange(seq)
    outs = []
    for gi, win in enumerate(POOL_WINDOWS):
        lo = win // 2
        hi = win - lo
        start = jnp.clip(pos - lo, 0, seq)
        end = jnp.clip(pos + hi, 0, seq)
        cg = csum[:, :, gi]
        cnt = (end - start).astype(jnp.float32)[None, :, None]
        outs.append((cg[:, end] - cg[:, start]) / cnt - uf[:, :, gi])
    pooled = jnp.stack(outs, axis=2).astype(u.dtype)
    mixed = jnp.einsum("blgc,gcd->blgd", pooled, w_pool)
    return mixed.reshape(bsz, seq, POOL_WIDTH) * pool_scale

def expert_choice_ffn(h, w_router, w_gate, w_up, w_down):
    bsz, seq, d = h.shape
    t = h.reshape(bsz * seq, d)
    n_tok = bsz * seq
    cap = CAPACITY_FACTOR * n_tok // N_EXPERTS
    probs = jax.nn.softmax(t.astype(jnp.float32) @ w_router.astype(jnp.float32), axis=-1)
    aff, idx = lax.top_k(probs.T, cap)
    xe = t[idx]
    hid = jax.nn.silu(jnp.einsum("ecd,edf->ecf", xe, w_gate)) * jnp.einsum("ecd,edf->ecf", xe, w_up)
    ye = jnp.einsum("ecf,efd->ecd", hid, w_down) * aff[..., None].astype(h.dtype)
    out = jnp.zeros_like(t).at[idx.reshape(-1)].add(ye.reshape(-1, d))
    return out.reshape(bsz, seq, d)

def encoder_layer(x, norm_mix_w, w_in, conv_w, conv_b, dt_bias_f, dt_bias_b, a_log_f, a_log_b,
                  d_skip, ssm_norm_w, w_ssm_out, w_pool, pool_scale, w_o, norm_ffn_w,
                  w_router, w_gate, w_up, w_down):
    h = rms_norm(x, norm_mix_w)
    proj = h @ w_in
    o1 = D_INNER
    o2 = o1 + CONV_CH
    o3 = o2 + SSM_HEADS
    o4 = o3 + SSM_HEADS
    o5 = o4 + POOL_WIDTH
    o6 = o5 + D_MODEL
    z, xbc, dt_f, dt_b, u_pool, g_a, g_b = jnp.split(proj, [o1, o2, o3, o4, o5, o6], axis=-1)
    y_a = ssd_branch(z, xbc, dt_f, dt_b, conv_w, conv_b, dt_bias_f, dt_bias_b,
                     a_log_f, a_log_b, d_skip, ssm_norm_w, w_ssm_out)
    y_b = pool_branch(u_pool, w_pool, pool_scale)
    merged = jax.nn.sigmoid(g_a) * y_a + jax.nn.sigmoid(g_b) * y_b
    x = x + merged @ w_o
    x = x + expert_choice_ffn(rms_norm(x, norm_ffn_w), w_router, w_gate, w_up, w_down)
    return x

def setup_inputs(seed: int = 0) -> dict:
    key = jax.random.key(seed)
    ks = jax.random.split(key, 24)
    f32 = jnp.float32

    def nrm(k, shape, scale):
        return jax.random.normal(k, shape, f32) * scale

    x_prompt = nrm(ks[0], (BATCH, SEQ, D_MODEL), 1.0)
    x_sample = nrm(ks[1], (DEC_BATCH, DEC_SEQ, D_MODEL), 1.0)
    norm_mix_w = 1.0 + nrm(ks[2], (DEPTH, D_MODEL), 0.02)
    w_in = nrm(ks[3], (DEPTH, D_MODEL, IN_COLS), D_MODEL ** -0.5)
    conv_w = nrm(ks[4], (DEPTH, CONV_K, CONV_CH), CONV_K ** -0.5)
    conv_b = nrm(ks[5], (DEPTH, CONV_CH), 0.02)
    dt_init = jnp.exp(jax.random.uniform(ks[6], (2, DEPTH, SSM_HEADS), f32,
                                         math.log(DT_MIN), math.log(DT_MAX)))
    dt_bias = dt_init + jnp.log(-jnp.expm1(-dt_init))
    a_log = jnp.log(jax.random.uniform(ks[7], (2, DEPTH, SSM_HEADS), f32, 1.0, 16.0))
    d_skip = 1.0 + nrm(ks[8], (DEPTH, SSM_HEADS), 0.1)
    ssm_norm_w = 1.0 + nrm(ks[9], (DEPTH, D_INNER), 0.02)
    w_ssm_out = nrm(ks[10], (DEPTH, D_INNER, D_MODEL), D_INNER ** -0.5)
    w_pool = nrm(ks[11], (DEPTH, POOL_GROUPS, POOL_GROUP_DIM, POOL_GROUP_DIM), POOL_GROUP_DIM ** -0.5)
    pool_scale = 1.0 + nrm(ks[12], (DEPTH, POOL_WIDTH), 0.02)
    w_o = nrm(ks[13], (DEPTH, D_MODEL, D_MODEL), D_MODEL ** -0.5)
    norm_ffn_w = 1.0 + nrm(ks[14], (DEPTH, D_MODEL), 0.02)
    w_router = nrm(ks[15], (DEPTH, D_MODEL, N_EXPERTS), D_MODEL ** -0.5)
    w_gate = nrm(ks[16], (DEPTH, N_EXPERTS, D_MODEL, EXPERT_FF), D_MODEL ** -0.5)
    w_up = nrm(ks[17], (DEPTH, N_EXPERTS, D_MODEL, EXPERT_FF), D_MODEL ** -0.5)
    w_down = nrm(ks[18], (DEPTH, N_EXPERTS, EXPERT_FF, D_MODEL), EXPERT_FF ** -0.5)
    norm_final_w = 1.0 + nrm(ks[19], (D_MODEL,), 0.02)
    return {
        "x_prompt": x_prompt, "x_sample": x_sample,
        "norm_mix_w": norm_mix_w, "w_in": w_in, "conv_w": conv_w, "conv_b": conv_b,
        "dt_bias_f": dt_bias[0], "dt_bias_b": dt_bias[1],
        "a_log_f": a_log[0], "a_log_b": a_log[1], "d_skip": d_skip,
        "ssm_norm_w": ssm_norm_w, "w_ssm_out": w_ssm_out,
        "w_pool": w_pool, "pool_scale": pool_scale, "w_o": w_o,
        "norm_ffn_w": norm_ffn_w, "w_router": w_router,
        "w_gate": w_gate, "w_up": w_up, "w_down": w_down,
        "norm_final_w": norm_final_w,
    }

def reference(x_prompt, x_sample, norm_mix_w, w_in, conv_w, conv_b, dt_bias_f, dt_bias_b,
              a_log_f, a_log_b, d_skip, ssm_norm_w, w_ssm_out, w_pool, pool_scale, w_o,
              norm_ffn_w, w_router, w_gate, w_up, w_down, norm_final_w):
    def trunk(x):
        for i in range(DEPTH):
            x = encoder_layer(x, norm_mix_w[i], w_in[i], conv_w[i], conv_b[i],
                              dt_bias_f[i], dt_bias_b[i], a_log_f[i], a_log_b[i], d_skip[i],
                              ssm_norm_w[i], w_ssm_out[i], w_pool[i], pool_scale[i], w_o[i],
                              norm_ffn_w[i], w_router[i], w_gate[i], w_up[i], w_down[i])
        return rms_norm(x, norm_final_w)

    y_prompt = trunk(x_prompt)
    y_sample = trunk(x_sample)
    return (y_prompt, y_sample)


_drawn_inputs = setup_inputs


def setup_inputs(seed=0):
    import zlib

    import numpy as np

    out = dict(_drawn_inputs(seed))
    spreads = {}
    factors = {'conv_b': 2.965,
     'ssm_norm_w': 4.114,
     'pool_scale': 4.732,
     'norm_ffn_w': 3.979,
     'norm_final_w': 2.836}
    for name, (base, spread) in spreads.items():
        noise = np.random.default_rng([zlib.crc32(name.encode()), seed]).standard_normal(out[name].shape)
        drawn = base * np.exp(spread * noise) if base else spread * noise
        out[name] = __import__('jax').numpy.asarray(drawn.astype(out[name].dtype))
    for name, factor in factors.items():
        out[name] = (out[name] * factor).astype(out[name].dtype)
    return out
```

```python
from contextlib import ExitStack

import concourse.bass as bass
from concourse import mybir

F32 = mybir.dt.float32
F32R = mybir.dt.float32r
I32 = mybir.dt.int32
ALU = mybir.AluOpType
ACT = mybir.ActivationFunctionType
AX_X = mybir.AxisListType.X

P = 128
D = 1024
KD = D // P
SEQS = (512, 256)
T = sum(SEQS)
NT = T // P
NTP = SEQS[0] // P
G = 8
H = 4
HD = 64
GW = H * HD
NH = 2 * G * H
TAPS = 5
CONV_IN = 2 + SEQS[0] + 4 + SEQS[1] + 2
CONV_OUT = CONV_IN - (TAPS - 1)
NQ = 4
WINDOWS = (2, 4, 8, 16)
PB = 8
POOL_IN = PB + SEQS[0] + 2 * PB + SEQS[1] + PB
E = 16
CAPS = tuple(2 * s // E for s in SEQS)
SLOTS = sum(CAPS)
FT = 2816 // P
UNITS = (2,) * 5 + (1,) + (2,) * 5 + (1,)
NU = len(UNITS)
RAW = 3
UT = max(UNITS)
UW = UT * P * (2 * KD + KD)
EPS = 1e-6
ACUM, DT, DTDE, DS, DC = range(5)
LOG_TERMS = 9

STATE_STEPS = ((0, 3), (1, 2), (2, 1), (4, 5))
STATE_FROM = (None, 0, 1, None)
FWD_STATE = {1: 0, 2: 1, 3: 2, 5: 3}
BWD_STATE = {2: 0, 1: 1, 0: 2, 4: 3}


def chunk_col(c):
    return c * P + (4 if c >= NTP else 0)


def heads(ap):
    return ap.rearrange("p (h w) -> p h w", h=H)


def per_head(ap):
    return ap.unsqueeze(2).to_broadcast([P, H, HD])


class Steps:

    def __init__(self, eng, sem, base=0):
        self.eng, self.sem, self.base, self.n = eng, sem, base, 0

    def __call__(self, ins):
        ins.then_inc(self.sem, 1)
        self.n += 1
        self.eng.wait_ge(self.sem, self.base + self.n)


class Alloc:

    def __init__(self, nc, ctx):
        self.nc, self.ctx = nc, ctx

    def sb(self, name, shape, dt=F32):
        return self.ctx.enter_context(self.nc.sbuf_tensor(name, shape, dt))

    def ps(self, name, shape):
        return self.ctx.enter_context(self.nc.psum_tensor(name, shape, F32))

    def sem(self, name):
        return self.ctx.enter_context(self.nc.semaphore(name))

    def sems(self, *names):
        return [self.sem(n) for n in names]


def prepare(nc, A, cst, hT, head_tab, acs):
    with ExitStack() as ctx:
        a = Alloc(nc, ctx)
        ident, tri_f, tri_b, ones, neg_half = cst
        x = a.sb("x_rows", [P, NT, D])
        xT = a.sb("xT", [P, KD, T])
        sq = a.sb("sq", [P, 2, D])
        nmix = a.sb("nmix", [P, KD])
        ssq = a.sb("ssq", [P, NT])
        rstd = a.sb("rstd", [P, NT])
        diag = a.sb("diag", [P, NT, P])
        wdt = a.sb("wdt", [P, KD, NH])
        bias = a.sb("bias", [P, NH])
        alog = a.sb("alog", [P, NH])
        ea = a.sb("ea", [P, NH])
        v, r, e, z, q, p, dt, dA, acum, tot, tmp = (a.sb(f"h_{n}", [P, NT, NH])
                                                    for n in ("v", "r", "e", "z", "q", "p", "dt", "dA", "acum", "tot", "tmp"))
        dAd = a.sb("dAd", [P, 2, NT, G * H])
        acT = a.sb("acT", [G * H, 2, NT, P])
        p_bc = a.ps("p_bc", [P, 1024])
        p_dt = a.ps("p_dt", [P, 512])
        p_f = a.ps("p_f", [P, 512])
        p_b = a.ps("p_b", [P, 512])
        p_tot = a.ps("p_tot", [P, 512])
        p_T = a.ps("p_T", [P, 1024])
        m_x, m_xT, m_small, m_const, m_acs = a.sems("m_x", "m_xT", "m_small", "m_const", "m_acs")
        s_ssq, s_rstd, s_diag, s_bc, s_hT = a.sems("s_ssq", "s_rstd", "s_diag", "s_bc", "s_hT")
        s_dt, s_dve, s_act, s_cum, s_cumT, s_copy = a.sems("s_dt", "s_dve", "s_act", "s_cum", "s_cumT", "s_copy")
        s_neg, s_absv, s_ones, s_dA, s_de = a.sems("s_neg", "s_absv", "s_ones", "s_dA", "s_de")

        def cum(t):
            return t[:, 0:NT * NH].rearrange("p (c n) -> p c n", c=NT)

        def by_group(t):
            return t.rearrange("p c (g x) -> p g c x", g=G)

        def by_dir(t, d):
            return t.rearrange("p c (g d h) -> p c g d h", g=G, d=2)[:, :, :, d, :]

        block = ctx.enter_context(nc.Block())

        @block.sync
        def _(sp):
            sp.dma_start(x[:], A["x"].rearrange("t p n -> p t n")).then_inc(m_x, 16)
            sp.dma_start(xT[:], A["xT"]).then_inc(m_xT, 16)
            sp.dma_start(wdt[:], A["w_dt"]).then_inc(m_small, 16)
            sp.wait_ge(s_copy, 2)
            for d in range(2):
                sp.dma_start(acs.rearrange("(g d h) t -> d g h t", g=G, d=2)[d],
                             acT[:, d].rearrange("r c l -> r (c l)")).then_inc(m_acs, 16)
            sp.wait_ge(m_acs, 32)

        @block.gpsimd
        def _(pool):
            pool.memset(ones[:], 1.0).then_inc(s_ones, 1)
            pool.memset(neg_half[:], -0.5).then_inc(s_neg, 1)
            pool.wait_ge(s_ssq, NT)
            chain = Steps(pool, s_rstd)
            chain(pool.tensor_scalar(ssq[:], ssq[:], 1.0 / D, EPS, ALU.mult, ALU.add))
            pool.wait_ge(s_neg, 1)
            chain(pool.tensor_tensor(rstd[:], ssq[:], neg_half[:], ALU.pow))

        @block.scalar
        def _(act):
            act.dma_start(ident[:], A["ident"]).then_inc(m_const, 16)
            act.dma_start(tri_f[:], A["tri_f"]).then_inc(m_const, 16)
            act.dma_start(tri_b[:], A["tri_b"]).then_inc(m_const, 16)
            act.dma_start(nmix[:], A["norm_mix"]).then_inc(m_const, 16)
            act.dma_start(bias[:], A["dt_bias"].partition_broadcast(P)).then_inc(m_const, 16)
            act.dma_start(alog[:], A["a_log"].partition_broadcast(P)).then_inc(m_const, 16)
            act.wait_ge(m_x, 16)
            for c in range(NT):
                if c >= 2:
                    act.wait_ge(s_ssq, c - 1)
                act.activation(sq[:, c % 2, :], x[:, c, :], ACT.Square, accum_out=ssq[:, c:c + 1]).then_inc(s_ssq, 1)
            act.wait_ge(m_const, 96)
            act.activation(ea[:], alog[:], ACT.Exp).then_inc(s_act, 1)
            act.wait_ge(s_absv, 1)
            act.activation(e[:], e[:], ACT.Exp).then_inc(s_act, 1)
            for d, src in enumerate((p_bc, p_T)):
                act.wait_ge(s_cumT, d + 1)
                act.activation(acT[:, d].rearrange("r c l -> r (c l)"), src[0:G * H, 0:T], ACT.Copy).then_inc(s_copy, 1)
            act.wait_ge(s_de, 1)
            act.activation(v[:], v[:], ACT.Exp).then_inc(s_act, 1)
            act.activation(z[:], acum[:], ACT.Exp).then_inc(s_act, 1)
            act.activation(q[:], tot[:], ACT.Exp).then_inc(s_act, 1)

        @block.tensor
        def _(pe):
            pe.wait_ge(s_ones, 1)
            pe.wait_ge(s_diag, 1)
            for c in range(NT):
                mm = pe.matmul(p_bc[:, c * P:(c + 1) * P], ones[:], diag[:, c, :], start=True, stop=True)
            mm.then_inc(s_bc, 1)
            pe.wait_ge(s_hT, KD)
            pe.wait_ge(m_small, 16)
            for c in range(NT):
                for k in range(KD):
                    mm = pe.matmul(cum(p_dt)[:, c, :], hT[:, k, c * P:(c + 1) * P], wdt[:, k, :],
                                   start=(k == 0), stop=(k == KD - 1))
            mm.then_inc(s_dt, 1)
            pe.wait_ge(s_dA, 3)
            for c in range(NT):
                for t, w in ((p_f, tri_f), (p_b, tri_b), (p_tot, ones)):
                    mm = pe.matmul(cum(t)[:, c, :], w[:], dA[:, c, :], start=True, stop=True)
            mm.then_inc(s_cum, 1)
            for d, (t, w) in enumerate(((p_bc, tri_f), (p_T, tri_b))):
                for c in range(NT):
                    mm = pe.matmul(t[0:G * H, c * P:(c + 1) * P], dAd[:, d, c, :], w[:],
                                   start=True, stop=True)
                mm.then_inc(s_cumT, 1)

        @block.vector
        def _(dve):
            dve.wait_ge(m_const, 96)
            dve.wait_ge(s_rstd, 2)
            for c in range(NT):
                ins = dve.tensor_scalar(diag[:, c, :], ident[:], rstd[:, c:c + 1], None, ALU.mult)
            ins.then_inc(s_diag, 1)
            dve.wait_ge(m_xT, 16)
            dve.wait_ge(s_bc, 1)
            for k in range(KD):
                dve.scalar_tensor_tensor(out=hT[:, k, :], in0=xT[:, k, :], scalar=nmix[:, k:k + 1],
                                         in1=p_bc[:, 0:T], op0=ALU.mult, op1=ALU.mult).then_inc(s_hT, 1)
            dve.wait_ge(s_dt, 1)
            chain = Steps(dve, s_dve)
            chain(dve.tensor_tensor(v[:], cum(p_dt), bias[:].unsqueeze(1).to_broadcast([P, NT, NH]), ALU.add))
            dve.scalar_tensor_tensor(out=e[:], in0=v[:], scalar=-1.0, in1=v[:], op0=ALU.mult, op1=ALU.min)\
                .then_inc(s_absv, 1)
            chain(dve.tensor_scalar(r[:], v[:], 0.0, None, ALU.max))
            dve.wait_ge(s_act, 2)
            chain(dve.tensor_scalar(z[:], e[:], 2.0, None, ALU.add))
            chain(dve.reciprocal(p[:], z[:]))
            chain(dve.tensor_tensor(z[:], e[:], p[:], ALU.mult))
            chain(dve.tensor_tensor(q[:], z[:], z[:], ALU.mult))
            chain(dve.tensor_scalar(p[:], q[:], 1.0 / (2 * LOG_TERMS - 1), None, ALU.mult))
            for k in range(LOG_TERMS - 2, 0, -1):
                chain(dve.scalar_tensor_tensor(out=p[:], in0=p[:], scalar=1.0 / (2 * k + 1), in1=q[:],
                                               op0=ALU.add, op1=ALU.mult))
            chain(dve.scalar_tensor_tensor(out=p[:], in0=p[:], scalar=1.0, in1=z[:], op0=ALU.add, op1=ALU.mult))
            chain(dve.scalar_tensor_tensor(out=dt[:], in0=p[:], scalar=2.0, in1=r[:], op0=ALU.mult, op1=ALU.add))
            dve.scalar_tensor_tensor(out=dA[:], in0=dt[:], scalar=-1.0,
                                     in1=ea[:].unsqueeze(1).to_broadcast([P, NT, NH]),
                                     op0=ALU.mult, op1=ALU.mult).then_inc(s_dA, 1)
            dve.wait_ge(s_dA, 1)
            for d in range(2):
                dve.tensor_copy(dAd[:, d].rearrange("p c (g h) -> p c g h", g=G), by_dir(dA[:], d)).then_inc(s_dA, 1)
            dve.tensor_copy(head_tab[:, :, DT], by_group(dt[:]))
            dve.wait_ge(s_cum, 1)
            dve.tensor_copy(by_dir(acum[:], 0), by_dir(cum(p_f), 0))
            dve.tensor_copy(by_dir(acum[:], 1), by_dir(cum(p_b), 1))
            chain(dve.tensor_copy(tot[:], cum(p_tot)))
            dve.tensor_tensor(v[:], tot[:], acum[:], ALU.subtract).then_inc(s_de, 1)
            dve.tensor_copy(head_tab[:, :, ACUM], by_group(acum[:]))
            dve.wait_ge(s_act, 3)
            chain(dve.tensor_tensor(p[:], v[:], dt[:], ALU.mult))
            dve.tensor_copy(head_tab[:, :, DTDE], by_group(p[:]))
            dve.wait_ge(s_act, 5)
            dve.tensor_copy(head_tab[:, :, DS], by_group(z[:]))
            dve.tensor_copy(head_tab[:, :, DC], by_group(q[:]))


def mixer(nc, A, cst, hT, head_tab, acs, ys):
    with ExitStack() as ctx:
        a = Alloc(nc, ctx)
        ident, tri_f, tri_b, ones, neg_half = cst
        conv_tab = a.sb("conv_tab", [P, G, 4 * (TAPS + 1)])
        out_tab = a.sb("out_tab", [P, G, 2 + H])
        conv_par = a.sb("conv_par", [P, 4 * (TAPS + 1)])
        out_par = a.sb("out_par", [P, 2 + H])
        head_par = a.sb("head_par", [P, 5, NT, 2 * H])
        wx = a.sb("wx", [P, 4, KD, P])
        wz = a.sb("wz", [P, KD, GW])
        pad = a.sb("pad", [P, 4, CONV_IN])
        u = a.sb("u", [P, 4, CONV_OUT])
        th = a.sb("th", [P, 2, CONV_OUT])
        ct = a.sb("ct", [P, NT, P])
        xtok = a.sb("xtok", [P, NT, GW])
        btok = a.sb("btok", [P, NT, P])
        cbm = a.sb("cbm", [P, NT, 2, P])
        xdt = a.sb("xdt", [P, NT, 2, GW])
        xw = a.sb("xw", [P, NT, 2, GW])
        st = a.sb("st", [P, len(STATE_STEPS), 2, GW])
        stt = a.sb("stt", [P, 2, GW])
        bc = a.sb("bc", [P, 2, 2, H, P])
        dec = a.sb("dec", [P, 2, 2, H, P])
        zs = a.sb("zs", [P, NT, GW])
        y = a.sb("y", [P, NT, GW])
        off = a.sb("off", [P, 2, GW])
        sqj = a.sb("sqj", [P, GW])
        ssq = a.sb("ssqg", [P, NT])
        rstd = a.sb("rstdg", [P, NT])
        yt = a.sb("yt", [P, 2, T])

        pp = [a.ps(f"pp{i}", [P, 1024]) for i in range(2)]
        ptr = a.ps("ptr", [P, 3, P])
        pst = a.ps("pst", [P, 2, GW])
        poff = a.ps("poff", [P, 2, GW])
        pdy = a.ps("pdy", [P, 2 * GW])
        pdg, pyt = pdy[:, 0:GW], pdy[:, GW:2 * GW]
        pcb = pdy[:, 0:P]

        m_par, s_wz, s_ysp = a.sems("m_par", "s_wz", "s_ysp")
        s_wx = a.sems(*[f"s_wx{j}" for j in range(4)])
        s_bc = a.sems("s_bc0", "s_bc1")
        s_zero, s_go, s_hpar, s_cpar = a.sems("s_zero", "s_go", "s_hpar", "s_cpar")
        s_proj, s_pad, s_tap, s_conv, s_tanh, s_u = a.sems("s_proj", "s_pad", "s_tap", "s_conv", "s_tanh", "s_u")
        s_zt, s_zs = a.sems("s_zt", "s_zs")
        s_tr, s_xb, s_cbm, s_ct, s_xdt = a.sems("s_tr", "s_xb", "s_cbm", "s_ct", "s_xdt")
        s_ust, s_stm, s_st = a.sems("s_ust", "s_stm", "s_st")
        s_seg, s_exp, s_m, s_y = a.sems("s_seg", "s_exp", "s_m", "s_y")
        s_ycs, s_yc, s_yz = a.sems("s_ycs", "s_yc", "s_yz")
        s_sq, s_rs, s_yn, s_yt, s_yte = a.sems("s_sq", "s_rs", "s_yn", "s_yt", "s_yte")

        def is0(g):
            return isinstance(g, int) and g == 0

        block = ctx.enter_context(nc.Block())

        @block.sync
        def _(sp):
            sp.dma_start(conv_tab[:], A["conv_tab"]).then_inc(m_par, 16)
            sp.dma_start(out_tab[:], A["out_tab"]).then_inc(m_par, 16)
            for j in range(4):
                sp.dma_start(wx[:, j], A["w_x"][0, j]).then_inc(s_wx[j], 16)
            sp.dma_start(wz[:], A["w_z"][0]).then_inc(s_wz, 16)
            with sp.Fori(1, G) as g:
                for j in range(4):
                    sp.wait_ge(s_proj, 6 * g + (j - 5))
                    sp.dma_start(wx[:, j], A["w_x"][g, j]).then_inc(s_wx[j], 16)
                sp.wait_ge(s_proj, 6 * g)
                sp.dma_start(wz[:], A["w_z"][g]).then_inc(s_wz, 16)

        @block.gpsimd
        def _(pool):
            def load_bc(gs, c):
                if not (is0(gs) and c < 2):
                    pool.wait_ge(s_seg, 6 * gs + (c - 1))
                pool.dma_start(bc[:, c % 2].rearrange("p d h l -> p (d h) l"),
                               acs[bass.ds(gs * 2 * H, 2 * H), c * P:(c + 1) * P].partition_broadcast(P))\
                    .then_inc(s_bc[c % 2], 16)

            def ssd(gs):
                load_bc(gs, 0)
                load_bc(gs, 1)
                pool.wait_ge(s_u, 4 * gs + 4)
                if not is0(gs):
                    pool.wait_ge(s_y, 6 * gs)
                pool.sem_inc(s_go, 1)
                for lo, hi in ((0, NTP), (NTP, NT)):
                    col = chunk_col(lo)
                    ins = pool.tensor_copy(ct[:, lo:hi, :].rearrange("p c n -> p (c n)"),
                                           u[:, 3, col:col + (hi - lo) * P])
                ins.then_inc(s_ct, 1)
                pool.wait_ge(s_hpar, gs + 1)
                if not is0(gs):
                    pool.wait_ge(s_ust, 4 * gs)
                    pool.wait_ge(s_yt, 6 * gs)
                for c in range(NT):
                    pool.wait_ge(s_xb, 6 * gs + (c + 1))
                    for d in range(2):
                        for dst, kind in ((xdt, DT), (xw, DTDE)):
                            pool.tensor_tensor(heads(dst[:, c, d, :]), heads(xtok[:, c, :]),
                                               per_head(head_par[:, kind, c, d * H:(d + 1) * H]), ALU.mult)
                    pool.tensor_tensor(heads(y[:, c, :]), heads(xtok[:, c, :]), per_head(out_par[:, 2:2 + H]),
                                       ALU.mult).then_inc(s_xdt, 1)
                for c in range(2, NT):
                    load_bc(gs, c)
                pool.wait_ge(s_sq, 6 * gs + NT)
                pool.sem_inc(s_go, 1)
                rs = Steps(pool, s_rs, 2 * gs)
                rs(pool.tensor_scalar(ssq[:], ssq[:], 1.0 / GW, EPS, ALU.mult, ALU.add))
                rs(pool.tensor_tensor(rstd[:], ssq[:], neg_half[:], ALU.pow))

            pool.memset(pad[:], 0.0).then_inc(s_zero, 1)
            ssd(0)
            with pool.Fori(1, G) as gs:
                ssd(gs)

        @block.scalar
        def _(act):
            def to_pad(g, j):
                act.wait_ge(s_proj, 6 * g + (j + 1))
                if not is0(g):
                    act.wait_ge(s_conv, 4 * g + (j - 3))
                act.activation(pad[:, j, 2:2 + SEQS[0]], pp[j % 2][:, 0:SEQS[0]], ACT.Copy)
                act.activation(pad[:, j, 6 + SEQS[0]:6 + T], pp[j % 2][:, SEQS[0]:T], ACT.Copy).then_inc(s_pad, 1)

            def tanh_conv(g, j):
                act.wait_ge(s_conv, 4 * g + (j + 1))
                if not (is0(g) and j < 2):
                    act.wait_ge(s_u, 4 * g + (j - 1))
                act.activation(th[:, j % 2, :], u[:, j, :], ACT.Tanh).then_inc(s_tanh, 1)

            def tanh_z(g, j):
                lo, hi = (0, NTP) if j == 4 else (NTP, NT)
                act.wait_ge(s_proj, 6 * g + (j + 1))
                if not is0(g):
                    act.wait_ge(s_yz, 6 * g)
                act.activation(zs[:, lo:hi, :].rearrange("p c w -> p (c w)"), pp[j % 2][:, 0:(hi - lo) * GW],
                               ACT.Tanh, scale=0.5).then_inc(s_zt, 1)

            def rows(gs):
                if not is0(gs):
                    act.wait_ge(s_xdt, 6 * gs)
                    act.wait_ge(s_ust, 4 * gs)
                for c in range(NT):
                    act.wait_ge(s_tr, 6 * gs + (c + 1))
                    act.activation(xtok[:, c, :], ptr[:, 0:2, :].rearrange("p a b -> p (a b)"), ACT.Copy)
                    act.activation(btok[:, c, :], ptr[:, 2, :], ACT.Copy).then_inc(s_xb, 1)

            def decay(gs, c):
                act.wait_ge(s_seg, 6 * gs + (c + 1))
                act.activation(dec[:, c % 2], dec[:, c % 2], ACT.Exp).then_inc(s_exp, 1)

            def square(gs, c):
                act.wait_ge(s_yz, 6 * gs + (c + 1))
                if c == 0 and not is0(gs):
                    act.wait_ge(s_rs, 2 * gs)
                if not (is0(gs) and c == 0):
                    act.wait_ge(s_sq, 6 * gs + c)
                act.activation(sqj[:], y[:, c, :], ACT.Square, accum_out=ssq[:, c:c + 1]).then_inc(s_sq, 1)

            def y_out(gs):
                act.wait_ge(s_hpar, gs + 1)
                if not is0(gs):
                    act.wait_ge(s_ysp, 16 * gs)
                for c in range(NT):
                    act.wait_ge(s_yt, 6 * gs + (c + 1))
                    for i in range(2):
                        ins = act.activation(yt[:, i, c * P:(c + 1) * P], pyt[:, i * P:(i + 1) * P], ACT.Copy,
                                             scale=out_par[:, i:i + 1])
                    ins.then_inc(s_yte, 1)
                act.wait_ge(s_yte, 6 * gs + NT)
                act.dma_start(ys[gs], yt[:]).then_inc(s_ysp, 16)

            def both(g, gs):
                rows(gs)
                decay(gs, 0)
                decay(gs, 1)
                if g is not None:
                    to_pad(g, 0)
                    tanh_conv(g, 0)
                    to_pad(g, 1)
                square(gs, 0)
                decay(gs, 2)
                if g is not None:
                    tanh_conv(g, 1)
                square(gs, 1)
                decay(gs, 3)
                if g is not None:
                    to_pad(g, 2)
                square(gs, 2)
                decay(gs, 4)
                if g is not None:
                    tanh_conv(g, 2)
                square(gs, 3)
                decay(gs, 5)
                if g is not None:
                    to_pad(g, 3)
                square(gs, 4)
                if g is not None:
                    tanh_conv(g, 3)
                square(gs, 5)
                if g is not None:
                    tanh_z(g, 4)
                y_out(gs)
                if g is not None:
                    tanh_z(g, 5)

            act.wait_ge(s_zero, 1)
            for j in range(4):
                to_pad(0, j)
                tanh_conv(0, j)
            tanh_z(0, 4)
            tanh_z(0, 5)
            both(1, 0)
            with act.Fori(2, G) as g:
                both(g, g - 1)
            both(None, G - 1)
            act.wait_ge(s_ysp, 16 * G)

        @block.tensor
        def _(pe):
            def project(g, j):
                if j >= 2:
                    pe.wait_ge(s_pad, 4 * g + (j - 1))
                elif not is0(g):
                    pe.wait_ge(s_zs, 2 * g + (j - 1))
                if j < 4:
                    pe.wait_ge(s_wx[j], 16 * g + 16)
                    for n0, n1 in ((0, SEQS[0]), (SEQS[0], T)):
                        for k in range(KD):
                            mm = pe.matmul(pp[j % 2][:, n0:n1], wx[:, j, k, :], hT[:, k, n0:n1],
                                           start=(k == 0), stop=(k == KD - 1))
                else:
                    pe.wait_ge(s_wz, 16 * g + 16)
                    lo, hi = (0, NTP) if j == 4 else (NTP, NT)
                    for c in range(lo, hi):
                        for k in range(KD):
                            mm = pe.matmul(pp[j % 2][:, (c - lo) * GW:(c - lo + 1) * GW],
                                           hT[:, k, c * P:(c + 1) * P], wz[:, k, :],
                                           start=(k == 0), stop=(k == KD - 1))
                mm.then_inc(s_proj, 1)

            def turn(gs):
                pe.wait_ge(s_u, 4 * gs + 4)
                for c in range(NT):
                    if not (is0(gs) and c == 0):
                        pe.wait_ge(s_xb, 6 * gs + c)
                        pe.wait_ge(s_cbm, 6 * gs + c)
                    col = chunk_col(c)
                    for j in range(3):
                        pe.transpose(ptr[:, j, :], u[:, j, col:col + P], ident[:])
                    if c == 0 and not is0(gs):
                        pe.wait_ge(s_yte, 6 * gs)
                    pe.matmul(pcb, u[:, 2, col:col + P], u[:, 3, col:col + P], start=True, stop=True)\
                      .then_inc(s_tr, 1)

            def states(gs):
                pe.wait_ge(s_xdt, 6 * gs + NT)
                pe.wait_ge(s_xb, 6 * gs + NT)
                for k, chunks in enumerate(STATE_STEPS):
                    if not (is0(gs) and k == 0):
                        pe.wait_ge(s_st, 4 * gs + k)
                    for d, c in enumerate(chunks):
                        mm = pe.matmul(pst[:, d, :], btok[:, c, :], xw[:, c, d, :], start=True, stop=True)
                    mm.then_inc(s_ust, 1)

            def output(gs, c):
                if c == 0:
                    pe.wait_ge(s_ct, gs + 1)
                    pe.wait_ge(s_st, 4 * gs + 4)
                if not (is0(gs) and c == 0):
                    pe.wait_ge(s_yc, 6 * gs + c)
                if c in FWD_STATE:
                    pe.matmul(poff[:, 0, :], ct[:, c, :], st[:, FWD_STATE[c], 0, :], start=True, stop=True)
                if c in BWD_STATE:
                    pe.matmul(poff[:, 1, :], ct[:, c, :], st[:, BWD_STATE[c], 1, :], start=True, stop=True)
                pe.wait_ge(s_m, 6 * gs + (c + 1))
                for h in range(H):
                    for d in range(2):
                        mm = pe.matmul(pdg[:, h * HD:(h + 1) * HD], dec[:, c % 2, d, h, :],
                                       xdt[:, c, d, h * HD:(h + 1) * HD], start=(d == 0), stop=(d == 1))
                mm.then_inc(s_y, 1)

            def turn_y(gs):
                pe.wait_ge(s_yn, gs + 1)
                for c in range(NT):
                    if not (is0(gs) and c == 0):
                        pe.wait_ge(s_yte, 6 * gs + c)
                    for i in range(2):
                        mm = pe.transpose(pyt[:, i * P:(i + 1) * P], y[:, c, i * P:(i + 1) * P], ident[:])
                    mm.then_inc(s_yt, 1)

            def both(g, gs):
                turn(gs)
                if g is not None:
                    project(g, 0)
                states(gs)
                if g is not None:
                    project(g, 1)
                output(gs, 0)
                output(gs, 1)
                if g is not None:
                    project(g, 2)
                output(gs, 2)
                output(gs, 3)
                if g is not None:
                    project(g, 3)
                output(gs, 4)
                output(gs, 5)
                if g is not None:
                    project(g, 4)
                turn_y(gs)
                if g is not None:
                    project(g, 5)

            for j in range(6):
                project(0, j)
            both(1, 0)
            with pe.Fori(2, G) as g:
                both(g, g - 1)
            both(None, G - 1)

        @block.vector
        def _(dve):
            def conv(g, j):
                if j == 0 and not is0(g):
                    dve.wait_ge(s_tr, 6 * g)
                    dve.wait_ge(s_ct, g)
                dve.wait_ge(s_pad, 4 * g + (j + 1))
                w0 = j * (TAPS + 1)
                tap = Steps(dve, s_tap, (TAPS - 1) * (4 * g + j))
                tap(dve.tensor_scalar(u[:, j, :], pad[:, j, 0:CONV_OUT], conv_par[:, w0:w0 + 1],
                                      conv_par[:, w0 + TAPS:w0 + TAPS + 1], ALU.mult, ALU.add))
                for k in range(1, TAPS):
                    ins = dve.scalar_tensor_tensor(out=u[:, j, :], in0=pad[:, j, k:k + CONV_OUT],
                                                   scalar=conv_par[:, w0 + k:w0 + k + 1], in1=u[:, j, :],
                                                   op0=ALU.mult, op1=ALU.add)
                    if k < TAPS - 1:
                        tap(ins)
                ins.then_inc(s_conv, 1)

            def silu(g, j):
                dve.wait_ge(s_tanh, 4 * g + (j + 1))
                dve.wait_ge(s_conv, 4 * g + (j + 1))
                dve.scalar_tensor_tensor(out=u[:, j, :], in0=th[:, j % 2, :], scalar=1.0, in1=u[:, j, :],
                                         op0=ALU.add, op1=ALU.mult).then_inc(s_u, 1)

            def gate(g, j):
                lo, hi = (0, NTP) if j == 4 else (NTP, NT)
                dve.wait_ge(s_zt, 2 * g + (j - 3))
                flat = zs[:, lo:hi, :].rearrange("p c w -> p (c w)")
                dve.scalar_tensor_tensor(out=flat, in0=flat, scalar=1.0, in1=pp[j % 2][:, 0:(hi - lo) * GW],
                                         op0=ALU.add, op1=ALU.mult).then_inc(s_zs, 1)

            def conv_params(g):
                if not is0(g):
                    dve.wait_ge(s_conv, 4 * g)
                dve.tensor_scalar(conv_par[:].unsqueeze(1), conv_tab[:, bass.ds(g, 1), :], 0.5, None, ALU.mult)\
                   .then_inc(s_cpar, 1)
                dve.wait_ge(s_cpar, g + 1)

            def head_params(gs):
                if not is0(gs):
                    dve.wait_ge(s_xdt, 6 * gs)
                    dve.wait_ge(s_yte, 6 * gs)
                dve.tensor_copy(out_par[:].unsqueeze(1), out_tab[:, bass.ds(gs, 1), :])
                dve.tensor_copy(head_par[:].rearrange("p k c x -> p (k c x)").unsqueeze(1),
                                head_tab[:].rearrange("p g k c x -> p g (k c x)")[:, bass.ds(gs, 1), :])\
                   .then_inc(s_hpar, 1)
                dve.wait_ge(s_hpar, gs + 1)

            def masked_cb(gs):
                for c in range(NT):
                    dve.wait_ge(s_tr, 6 * gs + (c + 1))
                    dve.tensor_tensor(cbm[:, c, 0, :], pcb, tri_f[:], ALU.mult)
                    dve.tensor_tensor(cbm[:, c, 1, :], pcb, tri_b[:], ALU.mult).then_inc(s_cbm, 1)

            def seg(gs, c):
                dve.wait_ge(s_bc[c % 2], 48 * gs + 16 * (c // 2 + 1))
                if not (is0(gs) and c < 2):
                    dve.wait_ge(s_y, 6 * gs + (c - 1))
                for d in range(2):
                    for h in range(H):
                        ins = dve.tensor_scalar(dec[:, c % 2, d, h, :], bc[:, c % 2, d, h, :],
                                                head_par[:, ACUM, c, d * H + h:d * H + h + 1], 0.0,
                                                ALU.subtract, ALU.min)
                ins.then_inc(s_seg, 1)

            def decayed(gs, c):
                dve.wait_ge(s_exp, 6 * gs + (c + 1))
                dve.wait_ge(s_cbm, 6 * gs + (c + 1))
                for d in range(2):
                    ins = dve.tensor_tensor(dec[:, c % 2, d], dec[:, c % 2, d],
                                            cbm[:, c, d, :].unsqueeze(1).to_broadcast([P, H, P]), ALU.mult)
                ins.then_inc(s_m, 1)

            def carry(gs):
                if not is0(gs):
                    dve.wait_ge(s_y, 6 * gs)
                for k, chunks in enumerate(STATE_STEPS):
                    dve.wait_ge(s_ust, 4 * gs + (k + 1))
                    if STATE_FROM[k] is None:
                        dve.tensor_copy(st[:, k], pst[:]).then_inc(s_st, 1)
                        continue
                    dve.wait_ge(s_st, 4 * gs + k)
                    for d, c in enumerate(chunks):
                        ins = dve.tensor_tensor(heads(stt[:, d, :]), heads(st[:, STATE_FROM[k], d, :]),
                                                per_head(head_par[:, DC, c, d * H:(d + 1) * H]), ALU.mult)
                    ins.then_inc(s_stm, 1)
                    dve.wait_ge(s_stm, 2 * gs + k)
                    dve.tensor_tensor(st[:, k], stt[:], pst[:], ALU.add).then_inc(s_st, 1)

            N_YCS = sum(2 + (c in FWD_STATE) + (c in BWD_STATE) - 1 for c in range(NT))

            def combine(gs, c, ycs):
                dve.wait_ge(s_y, 6 * gs + (c + 1))
                dve.wait_ge(s_xdt, 6 * gs + (c + 1))
                dirs = [d for d, have in enumerate((FWD_STATE, BWD_STATE)) if c in have]
                for d in dirs:
                    ins = dve.tensor_tensor(heads(off[:, d, :]), heads(poff[:, d, :]),
                                            per_head(head_par[:, DS, c, d * H:(d + 1) * H]), ALU.mult)
                ins.then_inc(s_ycs, 1)
                ycs.n += 1
                ycs(dve.tensor_tensor(y[:, c, :], y[:, c, :], pdg, ALU.add))
                for d in dirs[:-1]:
                    ycs(dve.tensor_tensor(y[:, c, :], y[:, c, :], off[:, d, :], ALU.add))
                dve.tensor_tensor(y[:, c, :], y[:, c, :], off[:, dirs[-1], :], ALU.add).then_inc(s_yc, 1)
                dve.wait_ge(s_yc, 6 * gs + (c + 1))
                dve.wait_ge(s_zs, 2 * gs + 2)
                dve.scalar_tensor_tensor(out=y[:, c, :], in0=y[:, c, :], scalar=0.5, in1=zs[:, c, :],
                                         op0=ALU.mult, op1=ALU.mult).then_inc(s_yz, 1)

            def normed(gs):
                dve.wait_ge(s_rs, 2 * gs + 2)
                dve.wait_ge(s_yz, 6 * gs + NT)
                for c in range(NT):
                    ins = dve.tensor_scalar(y[:, c, :], y[:, c, :], rstd[:, c:c + 1], None, ALU.mult)
                ins.then_inc(s_yn, 1)

            def both(g, gs):
                if g is not None:
                    conv_params(g)
                head_params(gs)
                ycs = Steps(dve, s_ycs, N_YCS * gs)
                masked_cb(gs)
                seg(gs, 0)
                seg(gs, 1)
                if g is not None:
                    conv(g, 0)
                carry(gs)
                decayed(gs, 0)
                if g is not None:
                    silu(g, 0)
                decayed(gs, 1)
                combine(gs, 0, ycs)
                seg(gs, 2)
                if g is not None:
                    conv(g, 1)
                combine(gs, 1, ycs)
                seg(gs, 3)
                decayed(gs, 2)
                if g is not None:
                    silu(g, 1)
                decayed(gs, 3)
                combine(gs, 2, ycs)
                seg(gs, 4)
                if g is not None:
                    conv(g, 2)
                combine(gs, 3, ycs)
                seg(gs, 5)
                decayed(gs, 4)
                if g is not None:
                    silu(g, 2)
                decayed(gs, 5)
                combine(gs, 4, ycs)
                if g is not None:
                    conv(g, 3)
                combine(gs, 5, ycs)
                if g is not None:
                    silu(g, 3)
                    gate(g, 4)
                normed(gs)
                if g is not None:
                    gate(g, 5)
                assert ycs.n == N_YCS

            dve.wait_ge(m_par, 32)
            conv_params(0)
            for j in range(4):
                conv(0, j)
                silu(0, j)
            gate(0, 4)
            gate(0, 5)
            both(1, 0)
            with dve.Fori(2, G) as g:
                both(g, g - 1)
            both(None, G - 1)


def merge(nc, A, hT, ys, mT):
    with ExitStack() as ctx:
        a = Alloc(nc, ctx)
        yT = a.sb("yT", [P, G, 2, T])
        wg = a.sb("wg", [P, 6, KD, P])
        ws = a.sb("ws", [P, 2, 2 * G, P])
        wpl = a.sb("wpl", [P, 2, 2 * P])
        pscale = a.sb("pscale", [P, KD])
        icnt = a.sb("icnt", [P, T])
        up = a.sb("up", [P, 2, POOL_IN])
        win = [a.sb(f"win{i}", [P, 2, POOL_IN]) for i in range(2)]
        pooled = a.sb("pooled", [P, 2, T])
        ya = a.sb("ya", [P, 2, T])
        ta = a.sb("ta", [P, 2, T])
        mx = a.sb("mx", [P, 2, T])
        tb = a.sb("tb", [P, 2, T])
        pq = [a.ps(f"pq{i}", [P, 1024]) for i in range(4)]
        m_y, m_ps, m_ic = a.sems("m_y", "m_ps", "m_ic")
        s_wg = a.sems(*[f"s_wg{j}" for j in range(6)])
        s_ws = a.sems("s_ws0", "s_ws1")
        s_wp = a.sem("s_wp")
        s_mm, s_ev, s_zero, s_win, s_pool, s_half, s_out, s_mg = a.sems(
            "q_mm", "q_ev", "q_zero", "q_win", "q_pool", "q_half", "q_out", "q_mg")
        U, YA, GA, MX, GB = range(5)
        steps = sum(len(WINDOWS[:q + 1]) for q in range(NQ))

        block = ctx.enter_context(nc.Block())

        @block.sync
        def _(sp):
            sp.dma_start(pscale[:], A["pool_scale"]).then_inc(m_ps, 16)
            for q in range(NQ):
                for j in range(6):
                    if q:
                        order = (U, GA, GB)[j // 2]
                        sp.wait_ge(s_mm, 10 * (q - 1) + 2 * order + j % 2 + 1)
                    sp.dma_start(wg[:, j], A["w_g"][q, j]).then_inc(s_wg[j], 16)
                    if j == 1:
                        for i in range(2):
                            if q:
                                sp.wait_ge(s_mm, 10 * (q - 1) + 2 * YA + i + 1)
                            sp.dma_start(ws[:, i], A["w_s"][2 * q + i]).then_inc(s_ws[i], 16)
                        if q == 0:
                            sp.dma_start(yT[:], ys.rearrange("g p i t -> p g i t")).then_inc(m_y, 16)
                        else:
                            sp.wait_ge(s_mm, 10 * (q - 1) + 2 * MX + 2)
                        sp.dma_start(wpl[:], A["w_p"][q]).then_inc(s_wp, 16)
                        if q:
                            sp.wait_ge(s_pool, q)
                        sp.dma_start(icnt[:], A["icnt"][q].partition_broadcast(P)).then_inc(m_ic, 16)

        @block.tensor
        def _(pe):
            n = 0

            def product(lhs, rhs, count):
                nonlocal n
                if n >= 4:
                    pe.wait_ge(s_ev, n - 3)
                for n0, n1 in ((0, SEQS[0]), (SEQS[0], T)):
                    for k in range(count):
                        mm = pe.matmul(pq[n % 4][:, n0:n1], lhs(k), rhs(k)[:, n0:n1],
                                       start=(k == 0), stop=(k == count - 1))
                mm.then_inc(s_mm, 1)
                n += 1

            for q in range(NQ):
                for i in range(2):
                    pe.wait_ge(s_wg[i], 16 * (q + 1))
                    product(lambda k: wg[:, i, k, :], lambda k: hT[:, k, :], KD)
                pe.wait_ge(m_y, 16)
                for i in range(2):
                    pe.wait_ge(s_ws[i], 16 * (q + 1))
                    product(lambda k: ws[:, i, k, :], lambda k: yT[:, k // 2, k % 2, :], 2 * G)
                for i in range(2):
                    pe.wait_ge(s_wg[2 + i], 16 * (q + 1))
                    product(lambda k: wg[:, 2 + i, k, :], lambda k: hT[:, k, :], KD)
                pe.wait_ge(s_wp, 16 * (q + 1))
                pe.wait_ge(s_pool, q + 1)
                for i in range(2):
                    product(lambda k: wpl[:, k, i * P:(i + 1) * P], lambda k: pooled[:, k, :], 2)
                for i in range(2):
                    pe.wait_ge(s_wg[4 + i], 16 * (q + 1))
                    product(lambda k: wg[:, 4 + i, k, :], lambda k: hT[:, k, :], KD)

        @block.scalar
        def _(act):
            n = 0
            act.wait_ge(s_zero, 1)
            act.wait_ge(s_half, 1)
            for q in range(NQ):
                for kind in range(5):
                    if q and kind == U:
                        act.wait_ge(s_pool, q)
                    if q and kind == YA:
                        act.wait_ge(s_mg, q)
                    for i in range(2):
                        act.wait_ge(s_mm, n + 1)
                        src = pq[n % 4]
                        if kind == U:
                            act.activation(up[:, i, PB:PB + SEQS[0]], src[:, 0:SEQS[0]], ACT.Copy)
                            ins = act.activation(up[:, i, 3 * PB + SEQS[0]:3 * PB + T], src[:, SEQS[0]:T], ACT.Copy)
                        elif kind == YA:
                            ins = act.activation(ya[:, i, :], src[:, 0:T], ACT.Copy)
                        elif kind == MX:
                            ins = act.activation(mx[:, i, :], src[:, 0:T], ACT.Copy,
                                                 scale=pscale[:, 2 * q + i:2 * q + i + 1])
                        else:
                            dst = ta if kind == GA else tb
                            ins = act.activation(dst[:, i, :], src[:, 0:T], ACT.Tanh, scale=0.5)
                        ins.then_inc(s_ev, 1)
                        n += 1

        @block.gpsimd
        def _(pool):
            pool.memset(up[:], 0.0).then_inc(s_zero, 1)
            done = 0
            for q in range(NQ):
                pool.wait_ge(s_ev, 10 * q + 2)
                if q:
                    pool.wait_ge(s_pool, q)
                src, length = up, POOL_IN
                for s in range(q + 1):
                    shift = 1 << s
                    length -= shift
                    dst = win[s % 2]
                    if s:
                        pool.wait_ge(s_win, done)
                    pool.tensor_tensor(dst[:, :, 0:length], src[:, :, 0:length], src[:, :, shift:shift + length],
                                       ALU.add).then_inc(s_win, 1)
                    done += 1
                    src = dst

        @block.vector
        def _(dve):
            dve.wait_ge(m_ps, 16)
            dve.tensor_scalar(pscale[:], pscale[:], 0.5, None, ALU.mult).then_inc(s_half, 1)
            done = chained = merged = 0
            for q in range(NQ):
                done += q + 1
                dve.wait_ge(s_win, done)
                dve.wait_ge(s_ev, 10 * q + 2)
                dve.wait_ge(m_ic, 16 * (q + 1))
                if q:
                    dve.wait_ge(s_mm, 10 * (q - 1) + 2 * MX + 2)
                src, half = win[q % 2], WINDOWS[q] // 2
                parts = ((0, SEQS[0], PB), (SEQS[0], T, 3 * PB))
                for lo, hi, border in parts:
                    n = hi - lo
                    ins = dve.tensor_tensor(pooled[:, :, lo:hi], src[:, :, lo + border - half:lo + border - half + n],
                                            icnt[:, lo:hi].unsqueeze(1).to_broadcast([P, 2, n]), ALU.mult)
                ins.then_inc(s_out, 1)
                chained += 1
                dve.wait_ge(s_out, chained)
                for lo, hi, border in parts:
                    ins = dve.tensor_tensor(pooled[:, :, lo:hi], pooled[:, :, lo:hi],
                                            up[:, :, lo + border:hi + border], ALU.subtract)
                ins.then_inc(s_pool, 1)
                dve.wait_ge(s_ev, 10 * q + 2 * GA + 2)
                ins = dve.scalar_tensor_tensor(out=ya[:], in0=ta[:], scalar=1.0, in1=ya[:], op0=ALU.add, op1=ALU.mult)
                ins.then_inc(s_out, 1)
                dve.wait_ge(s_ev, 10 * q + 2 * GB + 2)
                ins = dve.scalar_tensor_tensor(out=mx[:], in0=tb[:], scalar=1.0, in1=mx[:], op0=ALU.add, op1=ALU.mult)
                ins.then_inc(s_out, 1)
                chained += 2
                dve.wait_ge(s_out, chained)
                dve.scalar_tensor_tensor(out=mT[:, 2 * q:2 * q + 2, :], in0=ya[:], scalar=0.5, in1=mx[:],
                                         op0=ALU.mult, op1=ALU.add).then_inc(s_mg, 1)


def router(nc, A, cst, mT, h2, xa, idx, aff):
    with ExitStack() as ctx:
        a = Alloc(nc, ctx)
        ident, tri_f, tri_b, ones, neg_half = cst
        wo = a.sb("wo", [P, KD, D])
        xin = a.sb("xin", [P, 2, D])
        x2 = a.sb("x2", [P, 2, D])
        hh = a.sb("hh", [P, 2, D])
        hhT = a.sb("hhT", [P, 2, KD, P])
        sq = a.sb("sq2", [P, D])
        nffn = a.sb("nffn", [P, D])
        wr = a.sb("wr", [P, KD, E])
        ssq = a.sb("ssq2", [P, NT])
        rstd = a.sb("rstd2", [P, NT])
        mxl = a.sb("mxl", [P, NT])
        den = a.sb("den", [P, NT])
        prob = a.sb("prob", [P, NT, E])
        ROWS = 32 + E
        pblk = a.sb("pblk", [P, NTP, ROWS])
        pt = a.sb("pt", [ROWS, SEQS[0]])
        work = a.sb("work", [ROWS, SEQS[0]])
        tops = a.sb("tops", [ROWS, CAPS[0] // 8, 8])
        thr, cap, above = (a.sb(n, [ROWS, 1]) for n in ("thr", "cap", "above"))
        gt, eq, rank, one = (a.sb(n, [ROWS, SEQS[0]]) for n in ("gt", "eq", "rank", "one"))
        posT = a.sb("posT", [P, NTP, ROWS])
        slot1 = a.sb("slot1", [P, CAPS[0]])
        tokid = a.sb("tokid", [P, NT])
        oh_p = a.sb("oh_p", [P, NTP, E, CAPS[0]])
        oh_s = a.sb("oh_s", [P, NT - NTP, E, CAPS[1]])
        pairs = a.sb("pairs", [P, NT, E, 2])
        p_o = [a.ps(f"p_o{i}", [P, 1024]) for i in range(2)]
        p_t = a.ps("p_t", [P, 1024])
        p_l = a.ps("p_l", [P, 512])
        p_s = a.ps("p_s", [P, 512])
        m_c, s_st, r_wo = a.sems("m_c", "r_st", "r_wo")
        s_x = a.sems("r_x0", "r_x1")
        s_xa = a.sems("r_xa0", "r_xa1")
        s_h2 = a.sems("r_h20", "r_h21")
        s_o, s_x2, s_sq, s_rs, s_h, s_t, s_ht, s_l, s_pr, s_mx, s_e = a.sems(
            "r_o", "r_x2", "r_sq", "r_rs", "r_h", "r_t", "r_ht", "r_l", "r_pr", "r_mx", "r_e")
        s_c, s_pb, s_pt, s_ch, s_pos, s_posT, s_oh, s_ia, s_init = a.sems(
            "r_c", "r_pb", "r_pt", "r_ch", "r_pos", "r_posT", "r_oh", "r_ia", "r_init")

        block = ctx.enter_context(nc.Block())

        @block.sync
        def _(sp):
            sp.dma_start(wo[:], A["w_o"]).then_inc(r_wo, 16)
            sp.dma_start(nffn[:], A["norm_ffn"].partition_broadcast(P)).then_inc(m_c, 16)
            sp.dma_start(wr[:], A["w_router"]).then_inc(m_c, 16)
            sp.dma_start(slot1[:], A["slot1"].partition_broadcast(P)).then_inc(m_c, 16)
            sp.dma_start(tokid[:], A["tokid"]).then_inc(m_c, 16)
            for t in range(2):
                sp.dma_start(xin[:, t, :], A["x"][t]).then_inc(s_x[t], 16)
            for t in range(NT):
                sp.wait_ge(s_x2, t + 1)
                sp.dma_start(xa[t * P:(t + 1) * P, :], x2[:, t % 2, :]).then_inc(s_xa[t % 2], 16)
                if t + 2 < NT:
                    sp.dma_start(xin[:, t % 2, :], A["x"][t + 2]).then_inc(s_x[t % 2], 16)
                sp.wait_ge(s_h, t + 1)
                sp.dma_start(h2[t * P:(t + 1) * P, :], hh[:, t % 2, :]).then_inc(s_h2[t % 2], 16)
            for s in s_xa + s_h2:
                sp.wait_ge(s, 16 * NT // 2)

        @block.tensor
        def _(pe):
            def route(t):
                pe.wait_ge(s_h, t + 1)
                if t:
                    pe.wait_ge(s_ht, t)
                for k in range(KD):
                    mm = pe.transpose(p_t[:, k * P:(k + 1) * P], hh[:, t % 2, k * P:(k + 1) * P], ident[:])
                mm.then_inc(s_t, 1)

            def logits(t):
                pe.wait_ge(s_ht, t + 1)
                for k in range(KD):
                    mm = pe.matmul(p_l[:, t * E:(t + 1) * E], hhT[:, t % 2, k, :], wr[:, k, :],
                                   start=(k == 0), stop=(k == KD - 1))
                mm.then_inc(s_l, 1)

            pe.wait_ge(m_c, 64)
            pe.wait_ge(r_wo, 16)
            for t in range(NT):
                if t >= 2:
                    pe.wait_ge(s_x2, t - 1)
                for n in range(2):
                    for k in range(KD):
                        mm = pe.matmul(p_o[t % 2][:, n * 512:(n + 1) * 512], mT[:, k, t * P:(t + 1) * P],
                                       wo[:, k, n * 512:(n + 1) * 512], start=(k == 0), stop=(k == KD - 1))
                mm.then_inc(s_o, 1)
                if t:
                    route(t - 1)
                if t > 1:
                    logits(t - 2)
            route(NT - 1)
            logits(NT - 2)
            logits(NT - 1)
            pe.wait_ge(s_pb, 1)
            for b in range(NTP):
                mm = pe.transpose(p_s[0:ROWS, b * P:(b + 1) * P], pblk[:, b, :], ident[:])
            mm.then_inc(s_pt, 1)
            pe.wait_ge(s_pos, 1)
            for b in range(NTP):
                mm = pe.transpose(p_t[:, b * ROWS:(b + 1) * ROWS], rank[:, b * P:(b + 1) * P], ident[0:ROWS, 0:ROWS])
            mm.then_inc(s_posT, 1)
            pe.wait_ge(s_oh, 1)
            for e in range(E):
                for b in range(NTP):
                    pe.matmul(p_l[0:CAPS[0], 2 * e:2 * e + 2], oh_p[:, b, e, :], pairs[:, b, e, :],
                              start=(b == 0), stop=(b == NTP - 1))
                for b in range(NT - NTP):
                    mm = pe.matmul(p_l[CAPS[0]:SLOTS, 2 * e:2 * e + 2], oh_s[:, b, e, :], pairs[:, NTP + b, e, :],
                                   start=(b == 0), stop=(b == NT - NTP - 1))
            mm.then_inc(s_ia, 1)

        @block.scalar
        def _(act):
            def softmax_exp(t):
                act.activation(prob[:, t, :], p_l[:, t * E:(t + 1) * E], ACT.Exp, bias=mxl[:, t:t + 1],
                               accum_out=den[:, t:t + 1]).then_inc(s_e, 1)

            for t in range(NT):
                act.wait_ge(s_x2, t + 1)
                if t:
                    act.wait_ge(s_sq, t)
                act.activation(sq[:], x2[:, t % 2, :], ACT.Square, accum_out=ssq[:, t:t + 1]).then_inc(s_sq, 1)
                if t:
                    act.wait_ge(s_t, t)
                    if t > 2:
                        act.wait_ge(s_l, t - 2)
                    act.activation(hhT[:, (t - 1) % 2].rearrange("p k n -> p (k n)"), p_t[:], ACT.Copy)\
                       .then_inc(s_ht, 1)
            act.wait_ge(s_t, NT)
            act.wait_ge(s_l, NT - 2)
            act.activation(hhT[:, (NT - 1) % 2].rearrange("p k n -> p (k n)"), p_t[:], ACT.Copy).then_inc(s_ht, 1)
            act.wait_ge(s_mx, NT)
            for t in range(NT):
                softmax_exp(t)

        @block.gpsimd
        def _(pool):
            pool.memset(one[:], 1.0)
            pool.memset(pblk[:], -1.0)
            pool.memset(thr[:], 0.0)
            pool.memset(cap[:], float(CAPS[1])).then_inc(s_init, 1)
            pool.wait_ge(s_init, 1)
            pool.memset(cap[0:32], float(CAPS[0])).then_inc(s_init, 1)
            for t in range(NT):
                pool.wait_ge(s_sq, t + 1)
                rs = Steps(pool, s_rs, 2 * t)
                rs(pool.tensor_scalar(ssq[:, t:t + 1], ssq[:, t:t + 1], 1.0 / D, EPS, ALU.mult, ALU.add))
                rs(pool.tensor_tensor(rstd[:, t:t + 1], ssq[:, t:t + 1], neg_half[:, 0:1], ALU.pow))

        @block.vector
        def _(dve):
            def norm(t):
                dve.wait_ge(s_rs, 2 * t + 2)
                if t >= 2:
                    dve.wait_ge(s_t, t - 1)
                    dve.wait_ge(s_h2[t % 2], 16 * (t // 2))
                dve.scalar_tensor_tensor(out=hh[:, t % 2, :], in0=x2[:, t % 2, :], scalar=rstd[:, t:t + 1],
                                         in1=nffn[:], op0=ALU.mult, op1=ALU.mult).then_inc(s_h, 1)

            dve.wait_ge(m_c, 64)
            for t in range(NT):
                dve.wait_ge(s_x[t % 2], 16 * (t // 2 + 1))
                dve.wait_ge(s_o, t + 1)
                if t >= 2:
                    dve.wait_ge(s_xa[t % 2], 16 * (t // 2))
                    dve.wait_ge(s_sq, t - 1)
                    dve.wait_ge(s_h, t - 1)
                dve.tensor_tensor(x2[:, t % 2, :], p_o[t % 2][:], xin[:, t % 2, :], ALU.add).then_inc(s_x2, 1)
                if t:
                    norm(t - 1)
            norm(NT - 1)
            dve.wait_ge(s_l, NT)
            for t in range(NT):
                dve.tensor_reduce(mxl[:, t:t + 1], p_l[:, t * E:(t + 1) * E], AX_X, ALU.max, negate=True)\
                   .then_inc(s_mx, 1)
            dve.wait_ge(s_e, NT)
            ch = Steps(dve, s_ch)
            ch(dve.reciprocal(den[:], den[:]))
            ch(dve.tensor_tensor(prob[:], prob[:], den[:].unsqueeze(2).to_broadcast([P, NT, E]), ALU.mult))
            dve.wait_ge(s_init, 2)
            dve.tensor_copy(pblk[:, :, 0:E], prob[:, 0:NTP, :])
            dve.tensor_copy(pblk[:, 0:NT - NTP, 32:ROWS], prob[:, NTP:NT, :]).then_inc(s_pb, 1)
            dve.tensor_copy(pairs[:, :, :, 0], tokid[:].unsqueeze(2).to_broadcast([P, NT, E]))
            dve.tensor_copy(pairs[:, :, :, 1], prob[:])
            dve.wait_ge(s_pt, 1)
            ch(dve.tensor_copy(pt[:], p_s[0:ROWS, :]))
            ch(dve.tensor_copy(work[:], pt[:]))
            for r in range(CAPS[0] // 8):
                ch(dve.max(tops[:, r, :], work[:]))
                if r < CAPS[0] // 8 - 1:
                    ch(dve.match_replace(work[:], tops[:, r, :], work[:], -2.0))
            dve.tensor_copy(thr[0:E, :], tops[0:E, CAPS[0] // 8 - 1, 7:8])
            ch(dve.tensor_copy(thr[32:ROWS, :], tops[32:ROWS, CAPS[1] // 8 - 1, 7:8]))
            ch(dve.tensor_scalar(gt[:], pt[:], thr[:], 0.0, ALU.is_gt, ALU.add, accum_out=above[:]))
            ch(dve.tensor_scalar(eq[:], pt[:], thr[:], None, ALU.is_equal))
            ch(dve.tensor_tensor_scan(rank[:], one[:], eq[:], 0.0, ALU.mult, ALU.add))
            ch(dve.tensor_tensor(above[:], cap[:], above[:], ALU.subtract))
            ch(dve.scalar_tensor_tensor(out=eq[:], in0=rank[:], scalar=above[:], in1=eq[:],
                                        op0=ALU.is_le, op1=ALU.mult))
            ch(dve.tensor_tensor(gt[:], gt[:], eq[:], ALU.add))
            ch(dve.tensor_tensor_scan(work[:], one[:], gt[:], 0.0, ALU.mult, ALU.add))
            dve.tensor_tensor(rank[:], work[:], gt[:], ALU.mult).then_inc(s_pos, 1)
            dve.wait_ge(s_posT, 1)
            ch(dve.tensor_copy(posT[:].rearrange("p b r -> p (b r)"), p_t[:, 0:NTP * ROWS]))
            for b in range(NTP):
                dve.tensor_tensor(oh_p[:, b], posT[:, b, 0:E].unsqueeze(2).to_broadcast([P, E, CAPS[0]]),
                                  slot1[:].unsqueeze(1).to_broadcast([P, E, CAPS[0]]), ALU.is_equal)
            for b in range(NT - NTP):
                ins = dve.tensor_tensor(oh_s[:, b], posT[:, b, 32:ROWS].unsqueeze(2).to_broadcast([P, E, CAPS[1]]),
                                        slot1[:, 0:CAPS[1]].unsqueeze(1).to_broadcast([P, E, CAPS[1]]), ALU.is_equal)
            ins.then_inc(s_oh, 1)
            dve.wait_ge(s_ia, 1)
            got = p_l[0:SLOTS, 0:2 * E].rearrange("p (e k) -> p e k", k=2)
            dve.tensor_copy(idx[:, 0:E], got[:, :, 0])
            dve.tensor_copy(idx[:, E:E + 1], got[:, 0:1, 0])
            dve.tensor_copy(aff[:], got[:, :, 1]).then_inc(s_c, 1)
            dve.wait_ge(s_c, 1)


def experts(nc, A, cst, h2, xa, idx, aff):
    with ExitStack() as ctx:
        a = Alloc(nc, ctx)
        ident = cst[0]
        raw = a.sb("raw", [P, RAW, UW])
        wh = a.sb("wh", [P, 2, UW], F32R)
        wl = a.sb("wl", [P, 2, UW], F32R)
        idx_g = a.sb("idx_g", [SLOTS, 1], I32)
        idx_s = a.sb("idx_s", [SLOTS, 1], I32)
        aff_c = a.sb("aff_c", [SLOTS, 1])
        xe = a.sb("xe", [SLOTS, D])
        xh = a.sb("xh", [P, KD * SLOTS], F32R)
        xl = a.sb("xl", [P, KD * SLOTS], F32R)
        tg = a.sb("tg", [SLOTS, 2, UT * P])
        hid = a.sb("hid", [SLOTS, 2, UT * P])
        hh = a.sb("hid_hi", [P, 2, UT * SLOTS], F32R)
        hl = a.sb("hid_lo", [P, 2, UT * SLOTS], F32R)
        ye = a.sb("ye", [SLOTS, D])
        p_gu = [a.ps(f"p_gu{i}", [P, 512]) for i in range(2)]
        p_h = [a.ps(f"p_h{i}", [P, 512]) for i in range(2)]
        p_x = a.ps("p_x", [P, 1024])
        p_y = a.ps("p_y", [P, 1024])
        s_raw = a.sems(*[f"e_raw{i}" for i in range(RAW)])
        s_wh, s_wl, s_gu, s_dn, s_hid, s_t, s_hl, s_xl, s_ye, s_free = a.sems(
            "e_wh", "e_wl", "e_gu", "e_dn", "e_hid", "e_t", "e_hl", "e_xl", "e_ye", "e_free")
        s_tg, s_sg, s_hh, s_ig, s_is, s_g, s_xt, s_xh, s_sc, s_aff = a.sems(
            "e_tg", "e_sg", "e_hh", "e_ig", "e_is", "e_g", "e_xt", "e_xh", "e_sc", "e_aff")
        s_go = a.sem("e_go")
        W0 = 3 * RAW

        DOWN = UT * P * 2 * KD

        def pieces(nt):
            gu, dn = nt * P * 2 * KD, nt * P * KD
            return ((0, gu // 2, 0), (gu // 2, gu, gu // 2), (gu, gu + dn, DOWN))

        def tiles(ap):
            return ap.rearrange("p (k s) -> p k s", k=KD)

        turned = p_x[:].rearrange("p (k s) -> p k s", k=KD)[:, :, 0:SLOTS]

        def following(e, u):
            return (e + 1, 0) if u == NU - 1 else (e, u + 1)

        block = ctx.enter_context(nc.Block())

        @block.sync
        def _(sp):
            with sp.Fori(0, E) as e:
                for u, nt in enumerate(UNITS):
                    n = NU * e + u
                    sp.wait_ge(s_wh, 3 * n + 3)
                    sp.wait_ge(s_wl, 3 * n + 3)
                    w = nt * P * 3 * KD
                    at = sum(UNITS[:u]) * P * 3 * KD * P
                    src = A["w_e"][bass.ds(e, 1), at:at + w * P].rearrange("e (p n) -> p (e n)", p=P)
                    sp.dma_start(raw[:, u % RAW, 0:w], src).then_inc(s_raw[u % RAW], 16)

        @block.gpsimd
        def _(pool):
            def gather(e):
                pool.tensor_copy(idx_g[:], idx[:, bass.ds(e, 1)]).then_inc(s_ig, 1)
                pool.wait_ge(s_ig, e + 1)
                pool.sem_inc(s_go, 1)
                pool.indirect_dma_start(xe[:], None, h2, bass.IndirectOffsetOnAxis(ap=idx_g[:, 0:1], axis=0))\
                    .then_inc(s_g, 16)

            pool.sem_inc(s_free, 1)
            gather(0)
            with pool.Fori(0, E) as e:
                pool.wait_ge(s_xt, e + 1)
                gather(e + 1)
                pool.tensor_copy(idx_s[:], idx[:, bass.ds(e, 1)]).then_inc(s_is, 1)
                pool.wait_ge(s_is, e + 1)
                pool.wait_ge(s_ye, e + 2)
                pool.sem_inc(s_go, 1)
                pool.indirect_dma_start(xa, bass.IndirectOffsetOnAxis(ap=idx_s[:, 0:1], axis=0), ye[:], None,
                                        compute_op=ALU.add).then_inc(s_sc, 16)
                pool.wait_ge(s_sc, 16 * e + 16)
                pool.sem_inc(s_free, 1)
            pool.wait_ge(s_g, 16 * (E + 1))

        @block.scalar
        def _(act):
            def high(e, u, k):
                n = NU * e + u
                if k == 0:
                    act.wait_ge(s_raw[u % RAW], (16 * NU // RAW) * e + 16 * (u // RAW + 1))
                    act.wait_ge(s_gu, n + 1)
                if k == 2:
                    act.wait_ge(s_dn, n + 1)
                lo, hi, at = pieces(UNITS[u])[k]
                act.activation(wh[:, u % 2, at:at + hi - lo], raw[:, u % RAW, lo:hi], ACT.Copy).then_inc(s_wh, 1)

            def expert(e, last):
                act.wait_ge(s_xt, e + 1)
                act.wait_ge(s_gu, NU * e + 2)
                act.activation(tiles(xh[:]), turned, ACT.Copy).then_inc(s_xh, 1)
                for u, nt in enumerate(UNITS):
                    n = NU * e + u
                    ahead = None if last and u == NU - 1 else following(e, u)
                    if ahead:
                        high(*ahead, 0)
                        high(*ahead, 1)
                    act.wait_ge(s_gu, n + 3)
                    act.wait_ge(s_hid, n + 1)
                    act.activation(tg[:, u % 2, 0:nt * P], p_gu[u % 2][0:SLOTS, 0:nt * P], ACT.Tanh, scale=0.5)\
                       .then_inc(s_tg, 1)
                    if ahead:
                        high(*ahead, 2)
                    act.wait_ge(s_t, n + 3)
                    act.wait_ge(s_dn, n + 1)
                    act.activation(hh[:, u % 2, 0:nt * SLOTS], p_h[u % 2][:, 0:nt * SLOTS], ACT.Copy)\
                       .then_inc(s_hh, 1)

            act.sem_inc(s_wh, W0)
            for k in range(3):
                high(0, 0, k)
            with act.Fori(0, E - 1) as e:
                expert(e, False)
            expert(E - 1, True)

        @block.vector
        def _(dve):
            def low(e, u, k):
                lo, hi, at = pieces(UNITS[u])[k]
                to = slice(at, at + hi - lo)
                dve.wait_ge(s_wh, 3 * (NU * e + u) + (W0 + k + 1))
                dve.tensor_tensor(wl[:, u % 2, to], raw[:, u % RAW, lo:hi], wh[:, u % 2, to].bitcast(F32),
                                  ALU.subtract).then_inc(s_wl, 1)

            def expert(e, last):
                dve.wait_ge(s_ye, e + 1)
                dve.tensor_copy(aff_c[:], aff[:, bass.ds(e, 1)]).then_inc(s_aff, 1)
                dve.wait_ge(s_xh, e + 1)
                dve.tensor_tensor(tiles(xl[:]), turned, tiles(xh[:].bitcast(F32)), ALU.subtract).then_inc(s_xl, 1)
                for u, nt in enumerate(UNITS):
                    n = NU * e + u
                    w = nt * P
                    ahead = None if last and u == NU - 1 else following(e, u)
                    if ahead:
                        low(*ahead, 0)
                        low(*ahead, 1)
                    dve.wait_ge(s_tg, n + 1)
                    dve.scalar_tensor_tensor(out=tg[:, u % 2, 0:w], in0=tg[:, u % 2, 0:w], scalar=1.0,
                                             in1=p_gu[u % 2][0:SLOTS, 0:w], op0=ALU.add, op1=ALU.mult)\
                       .then_inc(s_sg, 1)
                    dve.wait_ge(s_sg, n + 1)
                    dve.wait_ge(s_t, n + 1)
                    dve.scalar_tensor_tensor(out=hid[:, u % 2, 0:w], in0=tg[:, u % 2, 0:w], scalar=0.5,
                                             in1=p_gu[u % 2][0:SLOTS, w:2 * w], op0=ALU.mult, op1=ALU.mult)\
                       .then_inc(s_hid, 1)
                    if ahead:
                        low(*ahead, 2)
                    dve.wait_ge(s_hh, n + 1)
                    dve.tensor_tensor(hl[:, u % 2, 0:nt * SLOTS], p_h[u % 2][:, 0:nt * SLOTS],
                                      hh[:, u % 2, 0:nt * SLOTS].bitcast(F32), ALU.subtract).then_inc(s_hl, 1)
                dve.wait_ge(s_aff, e + 1)
                dve.wait_ge(s_dn, NU * e + (NU + 2))
                dve.wait_ge(s_free, e + 1)
                dve.tensor_scalar(ye[:], p_y[0:SLOTS, :], aff_c[:], None, ALU.mult).then_inc(s_ye, 1)

            dve.sem_inc(s_wl, W0)
            dve.sem_inc(s_hid, 2)
            dve.sem_inc(s_hl, 2)
            dve.sem_inc(s_xl, 1)
            dve.sem_inc(s_ye, 1)
            for k in range(3):
                low(0, 0, k)
            with dve.Fori(0, E - 1) as e:
                expert(e, False)
            expert(E - 1, True)

        @block.tensor
        def _(pe):
            def gate_up(e, u, half):
                n = NU * e + u
                pe.wait_ge(s_wl, 3 * n + (W0 + half + 1))
                if half == 0:
                    pe.wait_ge(s_hid, n + 1)
                w = 2 * UNITS[u] * P
                for k in range(half * KD // 2, (half + 1) * KD // 2):
                    for i, (xx, ww) in enumerate(((xh, wh), (xl, wh), (xh, wl))):
                        mm = pe.matmul(p_gu[u % 2][0:SLOTS, 0:w], xx[:, k * SLOTS:(k + 1) * SLOTS],
                                       ww[:, u % 2, k * w:(k + 1) * w],
                                       start=(k == 0 and i == 0), stop=(k == KD - 1 and i == 2))
                if half == 1:
                    mm.then_inc(s_gu, 1)

            def turn(e, u):
                n = NU * e + u
                pe.wait_ge(s_hid, n + 3)
                pe.wait_ge(s_hl, n + 1)
                for i in range(UNITS[u]):
                    mm = pe.transpose(p_h[u % 2][:, i * SLOTS:(i + 1) * SLOTS], hid[:, u % 2, i * P:(i + 1) * P],
                                      ident[0:SLOTS, 0:SLOTS])
                mm.then_inc(s_t, 1)

            def down(e, u):
                n = NU * e + u
                nt = UNITS[u]
                if u == 0:
                    pe.wait_ge(s_ye, e + 1)
                pe.wait_ge(s_hl, n + 3)
                pe.wait_ge(s_wl, 3 * n + (W0 + 3))
                for i in range(nt):
                    for half in range(2):
                        for j, (hx, ww) in enumerate(((hh, wh), (hl, wh), (hh, wl))):
                            c0 = DOWN + i * D + half * 512
                            mm = pe.matmul(p_y[0:SLOTS, half * 512:(half + 1) * 512],
                                           hx[:, u % 2, i * SLOTS:(i + 1) * SLOTS], ww[:, u % 2, c0:c0 + 512],
                                           start=(u == 0 and i == 0 and j == 0),
                                           stop=(u == NU - 1 and i == nt - 1 and j == 2))
                mm.then_inc(s_dn, 1)

            pe.sem_inc(s_gu, 2)
            pe.sem_inc(s_dn, 2)
            pe.sem_inc(s_t, 2)
            with pe.Fori(0, E) as e:
                pe.wait_ge(s_g, 16 * e + 16)
                pe.wait_ge(s_xl, e + 1)
                for k in range(KD):
                    mm = pe.transpose(turned[:, k, :], xe[:, k * P:(k + 1) * P],
                                      ident[0:SLOTS, 0:SLOTS])
                mm.then_inc(s_xt, 1)
                pe.wait_ge(s_xl, e + 2)
                for u in range(NU):
                    gate_up(e, u, 0)
                    if u:
                        turn(e, u - 1)
                    gate_up(e, u, 1)
                    if u:
                        down(e, u - 1)
                turn(e, NU - 1)
                down(e, NU - 1)


def final(nc, A, cst, xa, outs):
    with ExitStack() as ctx:
        a = Alloc(nc, ctx)
        neg_half = cst[4]
        x = a.sb("xf", [P, NT, D])
        o = a.sb("of", [P, NT, D])
        sq = a.sb("sqf", [P, D])
        nfin = a.sb("nfin", [P, D])
        ssq = a.sb("ssqf", [P, NT])
        rstd = a.sb("rstdf", [P, NT])
        s_x = a.sems(*[f"f_x{t}" for t in range(NT)])
        s_n, s_sq, s_rs, s_o, s_out = a.sems("f_n", "f_sq", "f_rs", "f_o", "f_out")
        block = ctx.enter_context(nc.Block())

        @block.sync
        def _(sp):
            for t in range(NT):
                sp.dma_start(x[:, t, :], xa[t * P:(t + 1) * P, :]).then_inc(s_x[t], 16)
            sp.dma_start(nfin[:], A["norm_final"].partition_broadcast(P)).then_inc(s_n, 16)
            for t in range(NT):
                out, row = (outs[0], t * P) if t < NTP else (outs[1], (t - NTP) * P)
                sp.wait_ge(s_o, t + 1)
                sp.dma_start(out[0, row:row + P, :], o[:, t, :]).then_inc(s_out, 16)
            sp.wait_ge(s_out, 16 * NT)

        @block.scalar
        def _(act):
            for t in range(NT):
                act.wait_ge(s_x[t], 16)
                if t:
                    act.wait_ge(s_sq, t)
                act.activation(sq[:], x[:, t, :], ACT.Square, accum_out=ssq[:, t:t + 1]).then_inc(s_sq, 1)

        @block.gpsimd
        def _(pool):
            for t in range(NT):
                pool.wait_ge(s_sq, t + 1)
                rs = Steps(pool, s_rs, 2 * t)
                rs(pool.tensor_scalar(ssq[:, t:t + 1], ssq[:, t:t + 1], 1.0 / D, EPS, ALU.mult, ALU.add))
                rs(pool.tensor_tensor(rstd[:, t:t + 1], ssq[:, t:t + 1], neg_half[:, 0:1], ALU.pow))

        @block.vector
        def _(dve):
            dve.wait_ge(s_n, 16)
            for t in range(NT):
                dve.wait_ge(s_x[t], 16)
                dve.wait_ge(s_rs, 2 * t + 2)
                dve.scalar_tensor_tensor(out=o[:, t, :], in0=x[:, t, :], scalar=rstd[:, t:t + 1], in1=nfin[:],
                                         op0=ALU.mult, op1=ALU.mult).then_inc(s_o, 1)


def build(nc, A, outs):
    acs = nc.dram_tensor("acs", (G * 2 * H, T), F32).ap()
    ys = nc.dram_tensor("ys", (G, P, 2, T), F32).ap()
    h2 = nc.dram_tensor("h2", (T, D), F32).ap()
    xa = nc.dram_tensor("xa", (T, D), F32).ap()
    with ExitStack() as ctx:
        a = Alloc(nc, ctx)
        cst = [a.sb(n, [P, P]) for n in ("ident", "tri_f", "tri_b", "ones")] + [a.sb("neg_half", [P, NT])]
        idx = a.sb("idx", [SLOTS, E + 1], I32)
        aff = a.sb("aff", [SLOTS, E])
        with ExitStack() as mid:
            m = Alloc(nc, mid)
            hT = m.sb("hT", [P, KD, T])
            with ExitStack() as front:
                head_tab = Alloc(nc, front).sb("head_tab", [P, G, 5, NT, 2 * H])
                prepare(nc, A, cst, hT, head_tab, acs)
                mixer(nc, A, cst, hT, head_tab, acs, ys)
            mT = m.sb("mT", [P, KD, T])
            merge(nc, A, hT, ys, mT)
            router(nc, A, cst, mT, h2, xa, idx, aff)
        experts(nc, A, cst, h2, xa, idx, aff)
        final(nc, A, cst, xa, outs)


def kernel(**inputs):
    import numpy as np
    import concourse.bacc as _bacc
    from concourse import mybir as _mybir
    from concourse.bass_utils import run_bass_kernel_spmd as _run

    w = {k: np.asarray(v) for k, v in inputs.items()}
    x = np.concatenate([w["x_prompt"][0], w["x_sample"][0]])
    w_in = w["w_in"][0].reshape(KD, P, -1).transpose(1, 0, 2)
    di = G * GW
    o_x, o_B, o_C = di, 2 * di, 2 * di + G * P
    o_dt = o_C + G * P
    o_u, o_ga, o_gb = o_dt + NH, o_dt + NH + D, o_dt + NH + 2 * D
    z = w_in[:, :, :di].reshape(P, KD, G, GW)
    xs = w_in[:, :, o_x:o_B].reshape(P, KD, G, 2, P)
    b = w_in[:, :, o_B:o_C].reshape(P, KD, G, 1, P)
    c = w_in[:, :, o_C:o_dt].reshape(P, KD, G, 1, P)
    dtw = w_in[:, :, o_dt:o_u].reshape(P, KD, 2, G, H)
    pool_in = [w_in[:, :, o:o + D].reshape(P, KD, NQ, 2, P) for o in (o_u, o_ga, o_gb)]

    def by_head(f, bk):
        return np.stack([f, bk]).reshape(2, G, H).transpose(1, 0, 2).reshape(NH)

    taps = np.concatenate([w["conv_w"][0], w["conv_b"]])

    def tiles(a, off, n):
        return a[:, off:off + G * n * P].reshape(-1, G, n, P)
    cx, cb, cc = tiles(taps, 0, 2), tiles(taps, di, 1), tiles(taps, di + G * P, 1)
    conv_tab = np.concatenate([cx, cb, cc], axis=2).transpose(3, 1, 2, 0).reshape(P, G, -1)
    nw = w["ssm_norm_w"][0].reshape(G, 2, P).transpose(2, 0, 1)
    skip = np.broadcast_to(w["d_skip"][0].reshape(1, G, H), (P, G, H))
    gate = w["w_gate"][0].reshape(E, KD, P, FT, P)
    up = w["w_up"][0].reshape(E, KD, P, FT, P)
    down = w["w_down"][0].reshape(E, FT, P, D)
    w_e = np.empty((E, P * FT * P * 3 * KD), np.float32)
    t0 = at = 0
    for nt in UNITS:
        gu = np.stack([gate[:, :, :, t0:t0 + nt], up[:, :, :, t0:t0 + nt]], axis=3)
        gu = gu.transpose(0, 2, 1, 3, 4, 5).reshape(E, P, -1)
        dn = down[:, t0:t0 + nt].transpose(0, 2, 1, 3).reshape(E, P, -1)
        unit = np.concatenate([gu, dn], axis=2).reshape(E, -1)
        w_e[:, at:at + unit.shape[1]] = unit
        at += unit.shape[1]
        t0 += nt
    tri = np.tri(P, dtype=np.float32)
    counts = []
    for win in WINDOWS:
        for s in SEQS:
            pos = np.arange(s)
            n = np.clip(pos + win - win // 2, 0, s) - np.clip(pos - win // 2, 0, s)
            counts.append(1.0 / n)
    arrays = {
        "x": x.reshape(NT, P, D),
        "xT": x.T.reshape(KD, P, T).transpose(1, 0, 2),
        "norm_mix": w["norm_mix_w"][0].reshape(KD, P).T,
        "w_dt": dtw.transpose(0, 1, 3, 2, 4).reshape(P, KD, NH),
        "dt_bias": by_head(w["dt_bias_f"][0], w["dt_bias_b"][0]),
        "a_log": by_head(w["a_log_f"][0], w["a_log_b"][0]),
        "w_x": np.concatenate([xs, b, c], axis=3).transpose(2, 3, 0, 1, 4),
        "w_z": z.transpose(2, 0, 1, 3),
        "conv_tab": conv_tab,
        "out_tab": np.concatenate([nw, skip], axis=2),
        "w_g": np.concatenate(pool_in, axis=3).transpose(2, 3, 0, 1, 4),
        "w_s": w["w_ssm_out"][0].reshape(2 * G, P, KD, P).transpose(2, 1, 0, 3),
        "w_p": w["w_pool"][0].reshape(NQ, 2, P, 2 * P).transpose(0, 2, 1, 3),
        "pool_scale": w["pool_scale"][0].reshape(KD, P).T,
        "w_o": w["w_o"][0].reshape(KD, P, D).transpose(1, 0, 2),
        "norm_ffn": w["norm_ffn_w"][0],
        "w_router": w["w_router"][0].reshape(KD, P, E).transpose(1, 0, 2),
        "w_e": w_e,
        "norm_final": w["norm_final_w"],
        "ident": np.eye(P, dtype=np.float32),
        "tri_f": tri.T,
        "tri_b": tri,
        "icnt": np.concatenate(counts).reshape(NQ, T).astype(np.float32),
        "slot1": np.arange(1, CAPS[0] + 1, dtype=np.float32),
        "tokid": np.arange(T, dtype=np.float32).reshape(NT, P).T,
    }
    nc = _bacc.Bacc("TRN2", target_bir_lowering=False, num_devices=1)
    arrays = {f"in_{k}": np.ascontiguousarray(v) for k, v in arrays.items()}
    A = {k[3:]: nc.dram_tensor(k, v.shape, _mybir.dt.from_np(v.dtype), kind="ExternalInput").ap()
         for k, v in arrays.items()}
    outs = [nc.dram_tensor(f"out_{i}", (1, s, D), F32, kind="ExternalOutput").ap() for i, s in enumerate(SEQS)]
    build(nc, A, outs)
    r = _run(nc, [arrays], core_ids=[0])
    return tuple(r.results[0][f"out_{i}"] for i in range(len(SEQS)))
```

```python
from contextlib import ExitStack

import concourse.bass as bass
from concourse import mybir

F32 = mybir.dt.float32
F32R = mybir.dt.float32r
I32 = mybir.dt.int32
ALU = mybir.AluOpType
ACT = mybir.ActivationFunctionType
AX_X = mybir.AxisListType.X

P = 128
D = 1024
KD = D // P
SEQS = (512, 256)
T = sum(SEQS)
NT = T // P
NTP = SEQS[0] // P
G = 8
H = 4
HD = 64
GW = H * HD
NH = 2 * G * H
TAPS = 5
CONV_IN = 2 + SEQS[0] + 4 + SEQS[1] + 2
CONV_OUT = CONV_IN - (TAPS - 1)
PARTS = 4 * 3 + NT
NQ = 4
WINDOWS = (2, 4, 8, 16)
PB = 8
POOL_IN = PB + SEQS[0] + 2 * PB + SEQS[1] + PB
E = 16
CAPS = tuple(2 * s // E for s in SEQS)
SLOTS = sum(CAPS)
FT = 2816 // P
UNITS = (2,) * 5 + (1,) + (2,) * 5 + (1,)
NU = len(UNITS)
RAW = 3
UT = max(UNITS)
UW = UT * P * (2 * KD + KD)
EPS = 1e-6
ACUM, DT, DTDE, DS, DC = range(5)
LOG_TERMS = 9

DEC = 3

STATE_STEPS = ((0, 3), (1, 2), (2, 1), (4, 5))
STATE_FROM = (None, 0, 1, None)
FWD_STATE = {1: 0, 2: 1, 3: 2, 5: 3}
BWD_STATE = {2: 0, 1: 1, 0: 2, 4: 3}


def chunk_col(c):
    return c * P + (4 if c >= NTP else 0)


def heads(ap):
    return ap.rearrange("p (h w) -> p h w", h=H)


def three(a_hi, a_lo, b_hi, b_lo):
    return (a_hi, b_hi), (a_hi, b_lo), (a_lo, b_hi)


def per_head(ap):
    return ap.unsqueeze(2).to_broadcast([P, H, HD])


class Steps:

    def __init__(self, eng, sem, base=0):
        self.eng, self.sem, self.base, self.n = eng, sem, base, 0

    def __call__(self, ins):
        ins.then_inc(self.sem, 1)
        self.n += 1
        self.eng.wait_ge(self.sem, self.base + self.n)


class Alloc:

    def __init__(self, nc, ctx, clear=False):
        self.nc, self.ctx, self.clear, self.taken = nc, ctx, clear, []
        if clear:
            ctx.callback(lambda: (nc.clear_and_free_semaphores(self.taken), nc.all_engine_barrier()))

    def sb(self, name, shape, dt=F32):
        return self.ctx.enter_context(self.nc.sbuf_tensor(name, shape, dt))

    def ps(self, name, shape):
        return self.ctx.enter_context(self.nc.psum_tensor(name, shape, F32))

    def sem(self, name):
        if self.clear:
            self.taken.append(self.nc.alloc_semaphore(name))
            return self.taken[-1]
        return self.ctx.enter_context(self.nc.semaphore(name))

    def sems(self, *names):
        return [self.sem(n) for n in names]


def prepare(nc, A, cst, h_hi, h_lo, head_tab, acs):
    with ExitStack() as ctx:
        a = Alloc(nc, ctx, clear=True)
        ident, tri_f, tri_b, ones, neg_half = cst
        x = a.sb("x_rows", [P, NT, D])
        hT = a.sb("hT", [P, KD, T])
        xT = a.sb("xT", [P, KD, T])
        sq = a.sb("sq", [P, 2, D])
        nmix = a.sb("nmix", [P, KD])
        ssq = a.sb("ssq", [P, NT])
        rstd = a.sb("rstd", [P, NT])
        diag = a.sb("diag", [P, NT, P])
        wdt = a.sb("wdt", [P, KD, NH])
        bias = a.sb("bias", [P, NH])
        alog = a.sb("alog", [P, NH])
        ea = a.sb("ea", [P, NH])
        v, r, e, z, q, p, dt, dA, acum, tot = (a.sb(f"h_{n}", [P, NT, NH])
                                                    for n in ("v", "r", "e", "z", "q", "p", "dt", "dA", "acum", "tot"))
        dAd = a.sb("dAd", [P, 2, NT, G * H])
        acT = a.sb("acT", [G * H, 2, NT, P])
        p_bc = a.ps("p_bc", [P, 1024])
        p_dt = a.ps("p_dt", [P, 512])
        p_f = a.ps("p_f", [P, 512])
        p_b = a.ps("p_b", [P, 512])
        p_tot = a.ps("p_tot", [P, 512])
        p_T = a.ps("p_T", [P, 1024])
        m_x = a.sems(*[f"m_x{c}" for c in range(NT)])
        m_xT, m_small, m_const, m_acs = a.sems("m_xT", "m_small", "m_const", "m_acs")
        s_ssq, s_rstd, s_diag, s_bc, s_hT = a.sems("s_ssq", "s_rstd", "s_diag", "s_bc", "s_hT")
        s_dt, s_dve, s_act, s_cum, s_cumT, s_copy = a.sems("s_dt", "s_dve", "s_act", "s_cum", "s_cumT", "s_copy")
        s_hh = a.sem("s_hh")
        s_neg, s_absv, s_ones, s_dA, s_de = a.sems("s_neg", "s_absv", "s_ones", "s_dA", "s_de")

        def cum(t):
            return t[:, 0:NT * NH].rearrange("p (c n) -> p c n", c=NT)

        def by_group(t):
            return t.rearrange("p c (g x) -> p g c x", g=G)

        def by_dir(t, d):
            return t.rearrange("p c (g d h) -> p c g d h", g=G, d=2)[:, :, :, d, :]

        block = ctx.enter_context(nc.Block())

        @block.sync
        def _(sp):
            for c in range(NT):
                sp.dma_start(x[:, c], A["x"][c]).then_inc(m_x[c], 16)
            sp.dma_start(xT[:], A["xT"]).then_inc(m_xT, 16)
            sp.dma_start(wdt[:], A["w_dt"]).then_inc(m_small, 16)
            sp.wait_ge(s_copy, 2)
            for d in range(2):
                sp.dma_start(acs.rearrange("(g d h) t -> d g h t", g=G, d=2)[d],
                             acT[:, d].rearrange("r c l -> r (c l)")).then_inc(m_acs, 16)
            sp.wait_ge(m_acs, 32)

        @block.gpsimd
        def _(pool):
            pool.memset(ones[:], 1.0).then_inc(s_ones, 1)
            pool.memset(neg_half[:], -0.5).then_inc(s_neg, 1)
            pool.wait_ge(s_ssq, NT)
            chain = Steps(pool, s_rstd)
            chain(pool.tensor_scalar(ssq[:], ssq[:], 1.0 / D, EPS, ALU.mult, ALU.add))
            pool.wait_ge(s_neg, 1)
            chain(pool.tensor_tensor(rstd[:], ssq[:], neg_half[:], ALU.pow))

        @block.scalar
        def _(act):
            act.dma_start(ident[:], A["ident"]).then_inc(m_const, 16)
            act.dma_start(tri_f[:], A["tri_f"]).then_inc(m_const, 16)
            act.dma_start(tri_b[:], A["tri_b"]).then_inc(m_const, 16)
            act.dma_start(nmix[:], A["norm_mix"]).then_inc(m_const, 16)
            act.dma_start(bias[:], A["dt_bias"].partition_broadcast(P)).then_inc(m_const, 16)
            act.dma_start(alog[:], A["a_log"].partition_broadcast(P)).then_inc(m_const, 16)
            for c in range(NT):
                act.wait_ge(m_x[c], 16)
                if c >= 2:
                    act.wait_ge(s_ssq, c - 1)
                act.activation(sq[:, c % 2, :], x[:, c, :], ACT.Square, accum_out=ssq[:, c:c + 1]).then_inc(s_ssq, 1)
            act.wait_ge(m_const, 96)
            act.activation(ea[:], alog[:], ACT.Exp).then_inc(s_act, 1)
            for k in range(KD):
                act.wait_ge(s_hT, k + 1)
                act.activation(h_hi[:, k, :], hT[:, k, :], ACT.Copy).then_inc(s_hh, 1)
            act.wait_ge(s_absv, 1)
            act.activation(e[:], e[:], ACT.Exp).then_inc(s_act, 1)
            for d, src in enumerate((p_bc, p_T)):
                act.wait_ge(s_cumT, d + 1)
                act.activation(acT[:, d].rearrange("r c l -> r (c l)"), src[0:G * H, 0:T], ACT.Copy).then_inc(s_copy, 1)
            act.wait_ge(s_de, 1)
            act.activation(v[:], v[:], ACT.Exp).then_inc(s_act, 1)
            act.activation(z[:], acum[:], ACT.Exp).then_inc(s_act, 1)
            act.activation(q[:], tot[:], ACT.Exp).then_inc(s_act, 1)

        @block.tensor
        def _(pe):
            pe.wait_ge(s_ones, 1)
            pe.wait_ge(s_diag, 1)
            for c in range(NT):
                mm = pe.matmul(p_bc[:, c * P:(c + 1) * P], ones[:], diag[:, c, :], start=True, stop=True)
            mm.then_inc(s_bc, 1)
            pe.wait_ge(s_hT, KD)
            pe.wait_ge(m_small, 16)
            for c in range(NT):
                for k in range(KD):
                    mm = pe.matmul(cum(p_dt)[:, c, :], hT[:, k, c * P:(c + 1) * P], wdt[:, k, :],
                                   start=(k == 0), stop=(k == KD - 1))
            mm.then_inc(s_dt, 1)
            pe.wait_ge(s_dA, 3)
            for c in range(NT):
                for t, w in ((p_f, tri_f), (p_b, tri_b), (p_tot, ones)):
                    mm = pe.matmul(cum(t)[:, c, :], w[:], dA[:, c, :], start=True, stop=True)
            mm.then_inc(s_cum, 1)
            for d, (t, w) in enumerate(((p_bc, tri_f), (p_T, tri_b))):
                for c in range(NT):
                    mm = pe.matmul(t[0:G * H, c * P:(c + 1) * P], dAd[:, d, c, :], w[:],
                                   start=True, stop=True)
                mm.then_inc(s_cumT, 1)

        @block.vector
        def _(dve):
            dve.wait_ge(m_const, 96)
            dve.wait_ge(s_rstd, 2)
            for c in range(NT):
                ins = dve.tensor_scalar(diag[:, c, :], ident[:], rstd[:, c:c + 1], None, ALU.mult)
            ins.then_inc(s_diag, 1)
            dve.wait_ge(m_xT, 16)
            dve.wait_ge(s_bc, 1)
            for k in range(KD):
                dve.scalar_tensor_tensor(out=hT[:, k, :], in0=xT[:, k, :], scalar=nmix[:, k:k + 1],
                                         in1=p_bc[:, 0:T], op0=ALU.mult, op1=ALU.mult).then_inc(s_hT, 1)
            dve.wait_ge(s_dt, 1)
            chain = Steps(dve, s_dve)
            chain(dve.tensor_tensor(v[:], cum(p_dt), bias[:].unsqueeze(1).to_broadcast([P, NT, NH]), ALU.add))
            dve.scalar_tensor_tensor(out=e[:], in0=v[:], scalar=-1.0, in1=v[:], op0=ALU.mult, op1=ALU.min)\
                .then_inc(s_absv, 1)
            chain(dve.tensor_scalar(r[:], v[:], 0.0, None, ALU.max))
            for k in range(KD):
                dve.wait_ge(s_hh, k + 1)
                dve.tensor_tensor(h_lo[:, k, :], hT[:, k, :], h_hi[:, k, :].bitcast(F32), ALU.subtract)
            dve.wait_ge(s_act, 2)
            chain(dve.tensor_scalar(z[:], e[:], 2.0, None, ALU.add))
            chain(dve.reciprocal(p[:], z[:]))
            chain(dve.tensor_tensor(z[:], e[:], p[:], ALU.mult))
            chain(dve.tensor_tensor(q[:], z[:], z[:], ALU.mult))
            chain(dve.tensor_scalar(p[:], q[:], 1.0 / (2 * LOG_TERMS - 1), None, ALU.mult))
            for k in range(LOG_TERMS - 2, 0, -1):
                chain(dve.scalar_tensor_tensor(out=p[:], in0=p[:], scalar=1.0 / (2 * k + 1), in1=q[:],
                                               op0=ALU.add, op1=ALU.mult))
            chain(dve.scalar_tensor_tensor(out=p[:], in0=p[:], scalar=1.0, in1=z[:], op0=ALU.add, op1=ALU.mult))
            chain(dve.scalar_tensor_tensor(out=dt[:], in0=p[:], scalar=2.0, in1=r[:], op0=ALU.mult, op1=ALU.add))
            dve.scalar_tensor_tensor(out=dA[:], in0=dt[:], scalar=-1.0,
                                     in1=ea[:].unsqueeze(1).to_broadcast([P, NT, NH]),
                                     op0=ALU.mult, op1=ALU.mult).then_inc(s_dA, 1)
            dve.wait_ge(s_dA, 1)
            for d in range(2):
                dve.tensor_copy(dAd[:, d].rearrange("p c (g h) -> p c g h", g=G), by_dir(dA[:], d)).then_inc(s_dA, 1)
            dve.tensor_copy(head_tab[:, :, DT], by_group(dt[:]))
            dve.wait_ge(s_cum, 1)
            dve.tensor_copy(by_dir(acum[:], 0), by_dir(cum(p_f), 0))
            dve.tensor_copy(by_dir(acum[:], 1), by_dir(cum(p_b), 1))
            chain(dve.tensor_copy(tot[:], cum(p_tot)))
            dve.tensor_tensor(v[:], tot[:], acum[:], ALU.subtract).then_inc(s_de, 1)
            dve.tensor_copy(head_tab[:, :, ACUM], by_group(acum[:]))
            dve.wait_ge(s_act, 3)
            chain(dve.tensor_tensor(p[:], v[:], dt[:], ALU.mult))
            dve.tensor_copy(head_tab[:, :, DTDE], by_group(p[:]))
            dve.wait_ge(s_act, 5)
            dve.tensor_copy(head_tab[:, :, DS], by_group(z[:]))
            dve.tensor_copy(head_tab[:, :, DC], by_group(q[:]))


def mixer(nc, A, cst, h_hi, h_lo, head_tab, acs, ys):
    with ExitStack() as ctx:
        a = Alloc(nc, ctx)
        ident, tri_f, tri_b, ones, neg_half = cst
        conv_tab = a.sb("conv_tab", [P, G, 4 * (TAPS + 1)])
        skip_tab = a.sb("skip_tab", [P, G, H])
        conv_par = a.sb("conv_par", [P, 4 * (TAPS + 1)])
        skip = a.sb("skip", [P, H])
        head_par = a.sb("head_par", [P, 5, NT, 2 * H])
        raw = a.sb("w_raw", [P, 2, KD * P])
        wx_hi, wx_lo = (a.sb(n, [P, 2, KD * P], F32R) for n in ("wx_hi", "wx_lo"))
        wz_hi, wz_lo = (a.sb(n, [P, 2, KD * P], F32R) for n in ("wz_hi", "wz_lo"))
        pad = a.sb("pad", [P, 2, CONV_IN])
        u = a.sb("u", [P, 4, CONV_OUT])
        th = a.sb("th", [P, 2, CONV_OUT])
        ct = a.sb("ct", [P, NT, P])
        xtok = a.sb("xtok", [P, NT, GW])
        btok = a.sb("btok", [P, NT, P])
        cbm = a.sb("cbm", [P, NT, 2, P])
        xdt = a.sb("xdt", [P, NT, 2, GW])
        xw = a.sb("xw", [P, NT, 2, GW])
        zs = a.sb("zs", [P, NT, GW])
        y = a.sb("y", [P, NT, GW])
        dec = a.sb("dec", [P, DEC, 2, H, P])
        st = a.sb("st", [P, len(STATE_STEPS), 2, GW])
        off = a.sb("off", [P, 2, GW])
        stt = off
        sqj = a.sb("sqj", [P, GW])
        ssq = a.sb("ssqg", [P, NT])
        rstd = a.sb("rstdg", [P, NT])
        yt = a.sb("yt", [P, 2, T])

        pp = [a.ps(f"pp{i}", [P, 1024]) for i in range(2)]
        ptr = a.ps("ptr", [P, 3, P])
        pst = a.ps("pst", [P, 2, GW])
        poff = a.ps("poff", [P, 2, GW])
        pdg = a.ps("pdg", [P, GW])
        pyt = pst[:, 0, :]
        pstate = (pst, poff)
        pcb = (pdg[:, 0:P], poff[:, 0, 0:P])

        m_par, s_ysp, s_wh, s_wl = a.sems("m_par", "s_ysp", "s_wh", "s_wl")
        s_raw = a.sems("s_raw0", "s_raw1")
        s_bc = a.sems(*[f"s_bc{i}" for i in range(DEC)])
        s_zero, s_go, s_hpar, s_cpar = a.sems("s_zero", "s_go", "s_hpar", "s_cpar")
        s_proj, s_pad, s_tap, s_conv, s_tanh, s_u = a.sems("s_proj", "s_pad", "s_tap", "s_conv", "s_tanh", "s_u")
        s_zt, s_zs = a.sems("s_zt", "s_zs")
        s_tr, s_xb, s_cbm, s_ct, s_xdt = a.sems("s_tr", "s_xb", "s_cbm", "s_ct", "s_xdt")
        s_ust, s_stm, s_st = a.sems("s_ust", "s_stm", "s_st")
        s_seg, s_exp, s_m, s_y = a.sems("s_seg", "s_exp", "s_m", "s_y")
        s_ycs, s_yc, s_yz = a.sems("s_ycs", "s_yc", "s_yz")
        s_sq, s_rs, s_yn, s_yt, s_yte = a.sems("s_sq", "s_rs", "s_yn", "s_yt", "s_yte")

        def is0(g):
            return isinstance(g, int) and g == 0

        def unit(g, m, half):
            return ((wx_hi, wx_lo) if m < 4 else (wz_hi, wz_lo))[half][:, m % 2, :]

        block = ctx.enter_context(nc.Block())

        @block.sync
        def _(sp):
            sp.dma_start(conv_tab[:], A["conv_tab"]).then_inc(m_par, 16)
            sp.dma_start(skip_tab[:], A["d_skip"]).then_inc(m_par, 16)

            def load(g, m):
                if not (is0(g) and m < 2):
                    sp.wait_ge(s_wl, 6 * g + (m - 1))
                src = A["w_x"][bass.ds(g, 1), m].rearrange("g p n -> p (g n)")
                sp.dma_start(raw[:, m % 2], src).then_inc(s_raw[m % 2], 16)

            for m in range(6):
                load(0, m)
            with sp.Fori(1, G) as g:
                for m in range(6):
                    load(g, m)

        @block.gpsimd
        def _(pool):
            def load_bc(gs, c):
                if not (is0(gs) and c < DEC):
                    pool.wait_ge(s_y, 6 * gs + (c - DEC + 1))
                pool.dma_start(dec[:, c % DEC].rearrange("p d h l -> p (d h) l"),
                               acs[bass.ds(gs * 2 * H, 2 * H), c * P:(c + 1) * P].partition_broadcast(P))\
                    .then_inc(s_bc[c % DEC], 16)

            def ssd(gs):
                for c in range(DEC):
                    load_bc(gs, c)
                pool.wait_ge(s_u, 4 * gs + 4)
                if not is0(gs):
                    pool.wait_ge(s_y, 6 * gs)
                pool.sem_inc(s_go, 1)
                for lo, hi in ((0, NTP), (NTP, NT)):
                    col = chunk_col(lo)
                    ins = pool.tensor_copy(ct[:, lo:hi, :].rearrange("p c n -> p (c n)"),
                                           u[:, 3, col:col + (hi - lo) * P])
                ins.then_inc(s_ct, 1)
                pool.wait_ge(s_hpar, gs + 1)
                if not is0(gs):
                    pool.wait_ge(s_ust, 4 * gs)
                for c in range(NT):
                    pool.wait_ge(s_xb, 6 * gs + (c + 1))
                    for d in range(2):
                        for dst, kind in ((xdt, DT), (xw, DTDE)):
                            pool.tensor_tensor(heads(dst[:, c, d, :]), heads(xtok[:, c, :]),
                                               per_head(head_par[:, kind, c, d * H:(d + 1) * H]), ALU.mult)
                    if not is0(gs):
                        pool.wait_ge(s_yt, 6 * gs + (c - 5))
                    pool.tensor_tensor(heads(y[:, c, :]), heads(xtok[:, c, :]), per_head(skip[:]),
                                       ALU.mult).then_inc(s_xdt, 1)
                for c in range(DEC, NT):
                    load_bc(gs, c)
                pool.wait_ge(s_sq, 6 * gs + NT)
                pool.sem_inc(s_go, 1)
                rs = Steps(pool, s_rs, 2 * gs)
                rs(pool.tensor_scalar(ssq[:], ssq[:], 1.0 / GW, EPS, ALU.mult, ALU.add))
                rs(pool.tensor_tensor(rstd[:], ssq[:], neg_half[:], ALU.pow))

            pool.memset(pad[:], 0.0).then_inc(s_zero, 1)
            ssd(0)
            with pool.Fori(1, G) as gs:
                ssd(gs)

        @block.scalar
        def _(act):
            def high(g, m):
                act.wait_ge(s_raw[m % 2], 48 * g + 16 * (m // 2 + 1))
                if not is0(g) or m in (2, 3):
                    act.wait_ge(s_proj, 6 * g + (m - 3 if m < 2 else m - 1 if m < 4 else 0))
                act.activation(unit(g, m, 0), raw[:, m % 2], ACT.Copy).then_inc(s_wh, 1)

            def to_pad(g, j):
                act.wait_ge(s_proj, 6 * g + (j + 1))
                if not (is0(g) and j < 2):
                    act.wait_ge(s_conv, 4 * g + (j - 1))
                act.activation(pad[:, j % 2, 2:2 + SEQS[0]], pp[j % 2][:, 0:SEQS[0]], ACT.Copy)
                act.activation(pad[:, j % 2, 6 + SEQS[0]:6 + T], pp[j % 2][:, SEQS[0]:T], ACT.Copy)\
                   .then_inc(s_pad, 1)

            def tanh_conv(g, j):
                act.wait_ge(s_conv, 4 * g + (j + 1))
                if not (is0(g) and j < 2):
                    act.wait_ge(s_u, 4 * g + (j - 1))
                act.activation(th[:, j % 2, :], u[:, j, :], ACT.Tanh).then_inc(s_tanh, 1)

            def tanh_z(g, j):
                lo, hi = (0, NTP) if j == 4 else (NTP, NT)
                act.wait_ge(s_proj, 6 * g + (j + 1))
                if not is0(g):
                    act.wait_ge(s_yz, 6 * g + (hi - NT))
                act.activation(zs[:, lo:hi, :].rearrange("p c w -> p (c w)"), pp[j % 2][:, 0:(hi - lo) * GW],
                               ACT.Tanh, scale=0.5).then_inc(s_zt, 1)

            def rows(gs, c):
                if c == 0 and not is0(gs):
                    act.wait_ge(s_xdt, 6 * gs)
                    act.wait_ge(s_ust, 4 * gs)
                act.wait_ge(s_tr, 6 * gs + (c + 1))
                act.activation(xtok[:, c, :], ptr[:, 0:2, :].rearrange("p a b -> p (a b)"), ACT.Copy)
                act.activation(btok[:, c, :], ptr[:, 2, :], ACT.Copy).then_inc(s_xb, 1)

            def decay(gs, c):
                act.wait_ge(s_bc[c % DEC], 16 * NT // DEC * gs + 16 * (c // DEC + 1))
                act.wait_ge(s_hpar, gs + 1)
                for d in range(2):
                    for h in range(H):
                        x = d * H + h
                        ins = act.activation(dec[:, c % DEC, d, h, :], dec[:, c % DEC, d, h, :], ACT.Relu,
                                             scale=-1.0, bias=head_par[:, ACUM, c, x:x + 1])
                ins.then_inc(s_seg, 1)
                act.wait_ge(s_seg, 6 * gs + (c + 1))
                act.activation(dec[:, c % DEC], dec[:, c % DEC], ACT.Exp, scale=-1.0).then_inc(s_exp, 1)

            def square(gs, c):
                act.wait_ge(s_yz, 6 * gs + (c + 1))
                if c == 0 and not is0(gs):
                    act.wait_ge(s_rs, 2 * gs)
                if not (is0(gs) and c == 0):
                    act.wait_ge(s_sq, 6 * gs + c)
                act.activation(sqj[:], y[:, c, :], ACT.Square, accum_out=ssq[:, c:c + 1]).then_inc(s_sq, 1)

            def y_out(gy, c):
                if c == 0 and not is0(gy):
                    act.wait_ge(s_ysp, 16 * gy)
                act.wait_ge(s_yt, 6 * gy + (c + 1))
                act.activation(yt[:, :, c * P:(c + 1) * P], pyt.rearrange("p (i n) -> p i n", i=2), ACT.Copy)\
                   .then_inc(s_yte, 1)
                if c == NT - 1:
                    act.wait_ge(s_yte, 6 * gy + NT)
                    act.dma_start(ys[bass.ds(gy, 1)].rearrange("o p i t -> p (o i) t"), yt[:]).then_inc(s_ysp, 16)

            def both(g, gs, gy, more=True):
                def turned(c):
                    if gy is not None:
                        y_out(gy, c)
                    rows(gs, c)

                def ahead(step, j):
                    if g is not None:
                        step(g, j)

                turned(0)
                turned(1)
                decay(gs, 0)
                turned(2)
                ahead(to_pad, 0)
                ahead(high, 2)
                turned(3)
                decay(gs, 1)
                turned(4)
                turned(5)
                ahead(to_pad, 1)
                ahead(high, 3)
                decay(gs, 2)
                ahead(high, 4)
                ahead(tanh_conv, 0)
                ahead(tanh_conv, 1)
                ahead(high, 5)
                ahead(to_pad, 2)
                ahead(tanh_conv, 2)
                decay(gs, 3)
                square(gs, 0)
                ahead(to_pad, 3)
                if g is not None and more:
                    high(g + 1, 0)
                decay(gs, 4)
                square(gs, 1)
                ahead(tanh_conv, 3)
                if g is not None and more:
                    high(g + 1, 1)
                decay(gs, 5)
                square(gs, 2)
                square(gs, 3)
                square(gs, 4)
                ahead(tanh_z, 4)
                square(gs, 5)
                ahead(tanh_z, 5)

            act.wait_ge(s_zero, 1)
            high(0, 0)
            high(0, 1)
            for j in range(4):
                to_pad(0, j)
                high(0, j + 2)
                tanh_conv(0, j)
            high(1, 0)
            high(1, 1)
            tanh_z(0, 4)
            tanh_z(0, 5)
            both(1, 0, None)
            with act.Fori(2, G - 1) as g:
                both(g, g - 1, g - 2)
            both(G - 1, G - 2, G - 3, more=False)
            both(None, G - 1, G - 2)
            for c in range(NT):
                y_out(G - 1, c)
            act.wait_ge(s_ysp, 16 * G)

        @block.tensor
        def _(pe):
            def project(g, n):
                j, part = divmod(n, 3) if n < 12 else ((4, n - 12) if n < 16 else (5, n - 16))
                last = part == (2, 2, 2, 2, 3, 1)[j]
                if part == 0:
                    if j >= 2:
                        pe.wait_ge(s_pad, 4 * g + (j - 1))
                    elif not is0(g):
                        pe.wait_ge(s_zs, 2 * g + (j - 1))
                    pe.wait_ge(s_wl, 6 * g + min(j + 1, 5) + (j >= 4))
                if j < 4:
                    n0, n1 = (SEQS[0], T) if last else (0, SEQS[0])
                    ks = range(KD) if last else range(part * KD // 2, (part + 1) * KD // 2)
                    for k in ks:
                        for i, (w, h) in enumerate(three(wx_hi, wx_lo, h_hi, h_lo)):
                            mm = pe.matmul(pp[j % 2][:, n0:n1], w[:, j % 2, k * P:(k + 1) * P], h[:, k, n0:n1],
                                           start=(k == 0 and i == 0), stop=(k == KD - 1 and i == 2))
                else:
                    c = part + (0 if j == 4 else NTP)
                    for k in range(KD):
                        rows = slice(k % (KD // 2) * GW, (k % (KD // 2) + 1) * GW)
                        for i, (h, w) in enumerate(three(h_hi, h_lo, wz_hi, wz_lo)):
                            mm = pe.matmul(pp[j % 2][:, part * GW:(part + 1) * GW],
                                           h[:, k, c * P:(c + 1) * P], w[:, k // (KD // 2), rows],
                                           start=(k == 0 and i == 0), stop=(k == KD - 1 and i == 2))
                if last:
                    mm.then_inc(s_proj, 1)

            def turn(gs, c):
                if c == 0:
                    pe.wait_ge(s_u, 4 * gs + 4)
                    if not is0(gs):
                        pe.wait_ge(s_yc, 6 * gs)
                if not (is0(gs) and c == 0):
                    pe.wait_ge(s_xb, 6 * gs + c)
                if not (is0(gs) and c < 2):
                    pe.wait_ge(s_cbm, 6 * gs + (c - 1))
                col = chunk_col(c)
                for j in range(3):
                    pe.transpose(ptr[:, j, :], u[:, j, col:col + P], ident[:])
                pe.matmul(pcb[c % 2], u[:, 2, col:col + P], u[:, 3, col:col + P], start=True, stop=True)\
                  .then_inc(s_tr, 1)

            def states(gs, k):
                if k == 0:
                    pe.wait_ge(s_xdt, 6 * gs + NT)
                    pe.wait_ge(s_xb, 6 * gs + NT)
                    if not is0(gs):
                        pe.wait_ge(s_yte, 6 * gs)
                if k == 1:
                    pe.wait_ge(s_cbm, 6 * gs + NT)
                if not (is0(gs) and k < 2):
                    pe.wait_ge(s_st, 4 * gs + (k - 1))
                for d, c in enumerate(STATE_STEPS[k]):
                    mm = pe.matmul(pstate[k % 2][:, d, :], btok[:, c, :], xw[:, c, d, :], start=True, stop=True)
                mm.then_inc(s_ust, 1)

            def output(gs, c):
                if c == 0:
                    pe.wait_ge(s_ct, gs + 1)
                    pe.wait_ge(s_st, 4 * gs + 4)
                    pe.wait_ge(s_cbm, 6 * gs + NT)
                if not (is0(gs) and c == 0):
                    pe.wait_ge(s_yc, 6 * gs + c)
                if c in FWD_STATE:
                    pe.matmul(poff[:, 0, :], ct[:, c, :], st[:, FWD_STATE[c], 0, :], start=True, stop=True)
                if c in BWD_STATE:
                    pe.matmul(poff[:, 1, :], ct[:, c, :], st[:, BWD_STATE[c], 1, :], start=True, stop=True)
                pe.wait_ge(s_m, 6 * gs + (c + 1))
                for h in range(H):
                    for d in range(2):
                        mm = pe.matmul(pdg[:, h * HD:(h + 1) * HD], dec[:, c % DEC, d, h, :],
                                       xdt[:, c, d, h * HD:(h + 1) * HD], start=(d == 0), stop=(d == 1))
                mm.then_inc(s_y, 1)

            def turn_y(gy, c):
                if c == 0:
                    pe.wait_ge(s_yn, gy + 1)
                    pe.wait_ge(s_st, 4 * gy + 4)
                if not (is0(gy) and c == 0):
                    pe.wait_ge(s_yte, 6 * gy + c)
                for i in range(2):
                    mm = pe.transpose(pyt[:, i * P:(i + 1) * P], y[:, c, i * P:(i + 1) * P], ident[:])
                mm.then_inc(s_yt, 1)

            def both(g, gs, gy):
                steps = []
                for c in range(NT):
                    steps.append([(turn, gs, c)] if gy is None else [(turn_y, gy, c), (turn, gs, c)])
                steps.append([])
                steps += [[(states, gs, k)] for k in range(len(STATE_STEPS))]
                steps += [[(output, gs, c)] for c in range(NT)]
                for n in range(PARTS):
                    for step, group, m in steps[n] if n < len(steps) else ():
                        step(group, m)
                    if g is not None:
                        project(g, n)

            for n in range(PARTS):
                project(0, n)
            both(1, 0, None)
            with pe.Fori(2, G) as g:
                both(g, g - 1, g - 2)
            both(None, G - 1, G - 2)
            for c in range(NT):
                turn_y(G - 1, c)

        @block.vector
        def _(dve):
            def low(g, m):
                dve.wait_ge(s_wh, 6 * g + (m + 1))
                dve.tensor_tensor(unit(g, m, 1), raw[:, m % 2], unit(g, m, 0).bitcast(F32), ALU.subtract)\
                   .then_inc(s_wl, 1)

            def conv(g, j):
                if j == 0 and not is0(g):
                    dve.wait_ge(s_tr, 6 * g)
                    dve.wait_ge(s_ct, g)
                dve.wait_ge(s_pad, 4 * g + (j + 1))
                w0 = j * (TAPS + 1)
                tap = Steps(dve, s_tap, (TAPS - 1) * (4 * g + j))
                tap(dve.tensor_scalar(u[:, j, :], pad[:, j % 2, 0:CONV_OUT], conv_par[:, w0:w0 + 1],
                                      conv_par[:, w0 + TAPS:w0 + TAPS + 1], ALU.mult, ALU.add))
                for k in range(1, TAPS):
                    ins = dve.scalar_tensor_tensor(out=u[:, j, :], in0=pad[:, j % 2, k:k + CONV_OUT],
                                                   scalar=conv_par[:, w0 + k:w0 + k + 1], in1=u[:, j, :],
                                                   op0=ALU.mult, op1=ALU.add)
                    if k < TAPS - 1:
                        tap(ins)
                ins.then_inc(s_conv, 1)

            def silu(g, j):
                dve.wait_ge(s_tanh, 4 * g + (j + 1))
                dve.wait_ge(s_conv, 4 * g + (j + 1))
                dve.scalar_tensor_tensor(out=u[:, j, :], in0=th[:, j % 2, :], scalar=1.0, in1=u[:, j, :],
                                         op0=ALU.add, op1=ALU.mult).then_inc(s_u, 1)

            def gate(g, j):
                lo, hi = (0, NTP) if j == 4 else (NTP, NT)
                dve.wait_ge(s_zt, 2 * g + (j - 3))
                flat = zs[:, lo:hi, :].rearrange("p c w -> p (c w)")
                dve.scalar_tensor_tensor(out=flat, in0=flat, scalar=1.0, in1=pp[j % 2][:, 0:(hi - lo) * GW],
                                         op0=ALU.add, op1=ALU.mult).then_inc(s_zs, 1)

            def conv_params(g):
                if not is0(g):
                    dve.wait_ge(s_conv, 4 * g)
                dve.tensor_scalar(conv_par[:].unsqueeze(1), conv_tab[:, bass.ds(g, 1), :], 0.5, None, ALU.mult)\
                   .then_inc(s_cpar, 1)
                dve.wait_ge(s_cpar, g + 1)

            def head_params(gs):
                if not is0(gs):
                    dve.wait_ge(s_xdt, 6 * gs)
                    dve.wait_ge(s_exp, 6 * gs)
                dve.tensor_copy(skip[:].unsqueeze(1), skip_tab[:, bass.ds(gs, 1), :])
                dve.tensor_copy(head_par[:].rearrange("p k c x -> p (k c x)").unsqueeze(1),
                                head_tab[:].rearrange("p g k c x -> p g (k c x)")[:, bass.ds(gs, 1), :])\
                   .then_inc(s_hpar, 1)
                dve.wait_ge(s_hpar, gs + 1)

            def masked_cb(gs, c):
                dve.wait_ge(s_tr, 6 * gs + (c + 1))
                if c == 0 and not is0(gs):
                    dve.wait_ge(s_m, 6 * gs)
                dve.tensor_tensor(cbm[:, c, 0, :], pcb[c % 2], tri_f[:], ALU.mult)
                dve.tensor_tensor(cbm[:, c, 1, :], pcb[c % 2], tri_b[:], ALU.mult).then_inc(s_cbm, 1)

            def decayed(gs, c):
                dve.wait_ge(s_exp, 6 * gs + (c + 1))
                dve.wait_ge(s_cbm, 6 * gs + (c + 1))
                for d in range(2):
                    ins = dve.tensor_tensor(dec[:, c % DEC, d], dec[:, c % DEC, d],
                                            cbm[:, c, d, :].unsqueeze(1).to_broadcast([P, H, P]), ALU.mult)
                ins.then_inc(s_m, 1)

            def carry(gs, k):
                if k == 0 and not is0(gs):
                    dve.wait_ge(s_y, 6 * gs)
                dve.wait_ge(s_ust, 4 * gs + (k + 1))
                if STATE_FROM[k] is None:
                    dve.tensor_copy(st[:, k], pstate[k % 2][:]).then_inc(s_st, 1)
                    return
                dve.wait_ge(s_st, 4 * gs + k)
                for d, c in enumerate(STATE_STEPS[k]):
                    ins = dve.tensor_tensor(heads(stt[:, d, :]), heads(st[:, STATE_FROM[k], d, :]),
                                            per_head(head_par[:, DC, c, d * H:(d + 1) * H]), ALU.mult)
                ins.then_inc(s_stm, 1)
                dve.wait_ge(s_stm, 2 * gs + k)
                dve.tensor_tensor(st[:, k], stt[:], pstate[k % 2][:], ALU.add).then_inc(s_st, 1)

            N_YCS = sum(2 + (c in FWD_STATE) + (c in BWD_STATE) - 1 for c in range(NT))

            def combine(gs, c, ycs):
                dve.wait_ge(s_y, 6 * gs + (c + 1))
                dve.wait_ge(s_xdt, 6 * gs + (c + 1))
                dirs = [d for d, have in enumerate((FWD_STATE, BWD_STATE)) if c in have]
                for d in dirs:
                    ins = dve.tensor_tensor(heads(off[:, d, :]), heads(poff[:, d, :]),
                                            per_head(head_par[:, DS, c, d * H:(d + 1) * H]), ALU.mult)
                ins.then_inc(s_ycs, 1)
                ycs.n += 1
                ycs(dve.tensor_tensor(y[:, c, :], y[:, c, :], pdg[:], ALU.add))
                for d in dirs[:-1]:
                    ycs(dve.tensor_tensor(y[:, c, :], y[:, c, :], off[:, d, :], ALU.add))
                dve.tensor_tensor(y[:, c, :], y[:, c, :], off[:, dirs[-1], :], ALU.add).then_inc(s_yc, 1)
                dve.wait_ge(s_yc, 6 * gs + (c + 1))
                dve.wait_ge(s_zs, 2 * gs + 2)
                dve.scalar_tensor_tensor(out=y[:, c, :], in0=y[:, c, :], scalar=0.5, in1=zs[:, c, :],
                                         op0=ALU.mult, op1=ALU.mult).then_inc(s_yz, 1)

            def normed(gs):
                dve.wait_ge(s_rs, 2 * gs + 2)
                dve.wait_ge(s_yz, 6 * gs + NT)
                for c in range(NT):
                    ins = dve.tensor_scalar(y[:, c, :], y[:, c, :], rstd[:, c:c + 1], None, ALU.mult)
                ins.then_inc(s_yn, 1)

            def both(g, gs, more=True):
                ycs = Steps(dve, s_ycs, N_YCS * gs)

                def ahead(step, j):
                    if g is not None:
                        step(g, j)

                if g is not None:
                    conv_params(g)
                head_params(gs)
                masked_cb(gs, 0)
                masked_cb(gs, 1)
                decayed(gs, 0)
                masked_cb(gs, 2)
                ahead(low, 2)
                masked_cb(gs, 3)
                decayed(gs, 1)
                masked_cb(gs, 4)
                masked_cb(gs, 5)
                ahead(low, 3)
                ahead(conv, 0)
                carry(gs, 0)
                ahead(low, 4)
                ahead(silu, 0)
                carry(gs, 1)
                decayed(gs, 2)
                ahead(conv, 1)
                carry(gs, 2)
                carry(gs, 3)
                ahead(silu, 1)
                ahead(low, 5)
                ahead(conv, 2)
                ahead(silu, 2)
                combine(gs, 0, ycs)
                decayed(gs, 3)
                combine(gs, 1, ycs)
                ahead(conv, 3)
                combine(gs, 2, ycs)
                if g is not None and more:
                    low(g + 1, 0)
                decayed(gs, 4)
                ahead(silu, 3)
                if g is not None and more:
                    low(g + 1, 1)
                decayed(gs, 5)
                combine(gs, 3, ycs)
                combine(gs, 4, ycs)
                combine(gs, 5, ycs)
                ahead(gate, 4)
                normed(gs)
                ahead(gate, 5)
                assert ycs.n == N_YCS

            dve.wait_ge(m_par, 32)
            conv_params(0)
            low(0, 0)
            low(0, 1)
            for j in range(4):
                low(0, j + 2)
                conv(0, j)
                silu(0, j)
            low(1, 0)
            low(1, 1)
            gate(0, 4)
            gate(0, 5)
            both(1, 0)
            with dve.Fori(2, G - 1) as g:
                both(g, g - 1)
            both(G - 1, G - 2, more=False)
            both(None, G - 1)


def ssm_out(nc, A, ys, ya):
    with ExitStack() as ctx:
        a = Alloc(nc, ctx)
        y_raw = a.sb("y_raw", [P, 2, 2, T])
        y_hi, y_lo = (a.sb(n, [P, 2 * G, T], F32R) for n in ("y_hi", "y_lo"))
        raw = a.sb("ws_raw", [P, 2, KD * P])
        w_hi, w_lo = (a.sb(n, [P, 2, KD * P], F32R) for n in ("ws_hi", "ws_lo"))
        nw = a.sb("nw", [P, 2 * G])
        po = [a.ps(f"po{i}", [P, 1024]) for i in range(2)]
        m_nw, s_yh, s_yl, s_wh, s_wl, s_use, s_ev = a.sems(
            "o_nw", "o_yh", "o_yl", "o_wh", "o_wl", "o_use", "o_ev")
        s_y = a.sems("o_y0", "o_y1")
        s_raw = a.sems("o_raw0", "o_raw1")

        block = ctx.enter_context(nc.Block())

        @block.gpsimd
        def _(pool):
            for g in range(G):
                if g >= 2:
                    pool.wait_ge(s_yl, 2 * (g - 1))
                pool.dma_start(y_raw[:, g % 2], ys[g]).then_inc(s_y[g % 2], 16)

        @block.sync
        def _(sp):
            sp.dma_start(nw[:], A["ssm_norm"]).then_inc(m_nw, 16)
            with sp.Fori(0, KD) as i:
                for half in range(2):
                    sp.wait_ge(s_wl, 2 * i + (half + 1))
                    src = A["w_s"][bass.ds(2 * i + half, 1)].rearrange("u p n -> p (u n)")
                    sp.dma_start(raw[:, half], src).then_inc(s_raw[half], 16)

        @block.scalar
        def _(act):
            def high(i):
                for half in range(2):
                    act.wait_ge(s_raw[half], 16 * i + 16)
                    act.wait_ge(s_use, 2 * i + (half + 1))
                    act.activation(w_hi[:, half], raw[:, half], ACT.Copy).then_inc(s_wh, 1)

            def tile(i, s, last=False):
                if not last:
                    high(i + 1)
                act.wait_ge(s_use, 2 * i + 4)
                act.activation(ya[:, bass.ds(i, 1), :].rearrange("p o t -> p (o t)"), po[s][:, 0:T], ACT.Copy)\
                   .then_inc(s_ev, 1)

            act.sem_inc(s_ev, 2)
            high(0)
            act.wait_ge(m_nw, 16)
            for g in range(G):
                act.wait_ge(s_y[g % 2], 16 * (g // 2 + 1))
                for i in range(2):
                    act.activation(y_hi[:, 2 * g + i, :], y_raw[:, g % 2, i, :], ACT.Copy,
                                   scale=nw[:, 2 * g + i:2 * g + i + 1]).then_inc(s_yh, 1)
            with act.Fori(0, KD // 2 - 1) as it:
                tile(2 * it, 0)
                tile(2 * it + 1, 1)
            tile(KD - 2, 0)
            tile(KD - 1, 1, last=True)

        @block.vector
        def _(dve):
            def low(i):
                for half in range(2):
                    dve.wait_ge(s_wh, 2 * i + (half + 1))
                    dve.tensor_tensor(w_lo[:, half], raw[:, half], w_hi[:, half].bitcast(F32), ALU.subtract)\
                       .then_inc(s_wl, 1)

            dve.sem_inc(s_wl, 2)
            low(0)
            for g in range(G):
                for i in range(2):
                    dve.wait_ge(s_yh, 2 * g + i + 1)
                    dve.scalar_tensor_tensor(out=y_lo[:, 2 * g + i, :], in0=y_raw[:, g % 2, i, :],
                                             scalar=nw[:, 2 * g + i:2 * g + i + 1],
                                             in1=y_hi[:, 2 * g + i, :].bitcast(F32),
                                             op0=ALU.mult, op1=ALU.subtract).then_inc(s_yl, 1)
            with dve.Fori(1, KD) as i:
                low(i)

        @block.tensor
        def _(pe):
            pe.sem_inc(s_use, 2)
            with pe.Fori(0, KD // 2) as it:
                for s in range(2):
                    i = 2 * it + s
                    pe.wait_ge(s_ev, i + 1)
                    for half in range(2):
                        pe.wait_ge(s_wl, 2 * i + (half + 3))
                        for k in range(KD):
                            kk = half * KD + k
                            pe.wait_ge(s_yl, kk + 1)
                            for n0, n1 in ((0, SEQS[0]), (SEQS[0], T)):
                                for j, (w, y) in enumerate(three(w_hi, w_lo, y_hi, y_lo)):
                                    mm = pe.matmul(po[s][:, n0:n1], w[:, half, k * P:(k + 1) * P], y[:, kk, n0:n1],
                                                   start=(kk == 0 and j == 0), stop=(kk == 2 * KD - 1 and j == 2))
                        mm.then_inc(s_use, 1)


def gates(nc, A, h_hi, h_lo, ya, m_hi, m_lo):
    with ExitStack() as ctx:
        a = Alloc(nc, ctx)
        raw = a.sb("wg_raw", [P, 2, KD * P])
        w_hi, w_lo = (a.sb(n, [P, 2, KD * P], F32R) for n in ("wg_hi", "wg_lo"))
        pscale = a.sb("pscale", [P, KD])
        icnt = a.sb("icnt", [P, T])
        up = a.sb("up", [P, 2, POOL_IN])
        win = [a.sb(f"win{i}", [P, 2, POOL_IN]) for i in range(2)]
        pooled = a.sb("pooled", [P, 2, T])
        pl_hi, pl_lo = (a.sb(n, [P, 2, T], F32R) for n in ("pl_hi", "pl_lo"))
        tg = a.sb("t_gate", [P, 2, T])
        mx = a.sb("mx", [P, 2, T])
        pq = [a.ps(f"pq{i}", [P, 1024]) for i in range(4)]
        m_ps, m_ic = a.sems("q_ps", "q_ic")
        s_raw = a.sems("q_raw0", "q_raw1")
        s_wh, s_wl, s_mm, s_ev, s_zero, s_win, s_cnt, s_pool, s_ph, s_pl = a.sems(
            "q_wh", "q_wl", "q_mm", "q_ev", "q_zero", "q_win", "q_cnt", "q_pool", "q_ph", "q_pl")
        s_half, s_ga, s_gb, s_m, s_mh, s_ml = a.sems("q_half", "q_ga", "q_gb", "q_m", "q_mh", "q_ml")
        U, GA, MX, GB = range(4)
        ORDER = ((U, 0), (U, 1), (GA, 0), (GA, 1), (GB, 0), (MX, 0), (MX, 1), (GB, 1))
        NUN = 7
        MAP = 5
        TOTAL = NQ * NUN

        def products(m):
            q, j = divmod(m, NUN)
            return 8 * q + j + (2 if j >= MAP else 1)

        def width(m):
            return 4 * P if m % NUN == MAP else KD * P

        block = ctx.enter_context(nc.Block())

        @block.sync
        def _(sp):
            sp.dma_start(pscale[:], A["pool_scale"]).then_inc(m_ps, 16)
            for m in range(TOTAL):
                q, j = divmod(m, NUN)
                if m >= 2:
                    sp.wait_ge(s_wl, m - 1)
                src = A["w_p"][q] if j == MAP else A["w_g"][q, j if j < MAP else j - 1]
                sp.dma_start(raw[:, m % 2, 0:width(m)], src).then_inc(s_raw[m % 2], 16)
                if j == 1:
                    if q:
                        sp.wait_ge(s_cnt, q)
                    sp.dma_start(icnt[:], A["icnt"][q].partition_broadcast(P)).then_inc(m_ic, 16)

        @block.tensor
        def _(pe):
            n = m = 0

            def product(w, x, cols, ks):
                nonlocal n
                if n >= 4:
                    pe.wait_ge(s_ev, n - 3)
                for k in ks:
                    for n0, n1 in ((0, SEQS[0]), (SEQS[0], T)):
                        for j, (ww, xx) in enumerate(three(*w, *x)):
                            mm = pe.matmul(pq[n % 4][:, n0:n1], ww[:, m % 2, cols(k)], xx[:, k, n0:n1],
                                           start=(k == 0 and j == 0), stop=(k == ks[-1] and j == 2))
                mm.then_inc(s_mm, 1)
                n += 1

            for q in range(NQ):
                for kind, i in ORDER:
                    pe.wait_ge(s_wl, m + 1)
                    if kind == MX:
                        if i == 0:
                            pe.wait_ge(s_pl, q + 1)
                        product((w_hi, w_lo), (pl_hi, pl_lo),
                                lambda k: slice(k * 2 * P + i * P, k * 2 * P + (i + 1) * P), range(2))
                    else:
                        product((w_hi, w_lo), (h_hi, h_lo), lambda k: slice(k * P, (k + 1) * P), range(KD))
                    if (kind, i) != (MX, 0):
                        m += 1

        @block.scalar
        def _(act):
            def high(m):
                if m >= TOTAL:
                    return
                act.wait_ge(s_raw[m % 2], 16 * (m // 2 + 1))
                if m >= 2:
                    act.wait_ge(s_mm, products(m - 2))
                act.activation(w_hi[:, m % 2, 0:width(m)], raw[:, m % 2, 0:width(m)], ACT.Copy).then_inc(s_wh, 1)

            def take(q, kind, i):
                n = 8 * q + ORDER.index((kind, i))
                act.wait_ge(s_mm, n + 1)
                src = pq[n % 4]
                if kind == U:
                    act.activation(up[:, i, PB:PB + SEQS[0]], src[:, 0:SEQS[0]], ACT.Copy)
                    ins = act.activation(up[:, i, 3 * PB + SEQS[0]:3 * PB + T], src[:, SEQS[0]:T], ACT.Copy)
                elif kind == MX:
                    ins = act.activation(mx[:, i, :], src[:, 0:T], ACT.Copy, scale=pscale[:, 2 * q + i:2 * q + i + 1])
                else:
                    ins = act.activation(tg[:, i, :], src[:, 0:T], ACT.Tanh, scale=0.5)
                ins.then_inc(s_ev, 1)

            def result(q):
                act.wait_ge(s_m, q + 1)
                act.activation(m_hi[:, 2 * q:2 * q + 2, :], mx[:], ACT.Copy).then_inc(s_mh, 1)

            high(0)
            high(1)
            act.wait_ge(s_zero, 1)
            act.wait_ge(s_half, 1)
            for q in range(NQ):
                m = NUN * q
                if q:
                    act.wait_ge(s_pool, q)
                take(q, U, 0)
                high(m + 2)
                take(q, U, 1)
                high(m + 3)
                if q:
                    result(q - 1)
                    act.wait_ge(s_gb, q)
                take(q, GA, 0)
                high(m + 4)
                take(q, GA, 1)
                act.wait_ge(s_pool, q + 1)
                act.activation(pl_hi[:], pooled[:], ACT.Copy).then_inc(s_ph, 1)
                high(m + 5)
                act.wait_ge(s_ga, q + 1)
                take(q, GB, 0)
                high(m + 6)
                if q:
                    act.wait_ge(s_ml, q)
                take(q, MX, 0)
                take(q, MX, 1)
                high(m + 7)
                take(q, GB, 1)
                high(m + 8)
            result(NQ - 1)

        @block.gpsimd
        def _(pool):
            pool.memset(up[:], 0.0).then_inc(s_zero, 1)
            done = 0
            for q in range(NQ):
                pool.wait_ge(s_ev, 8 * q + 2)
                if q:
                    pool.wait_ge(s_pool, q)
                src, length = up, POOL_IN
                for s in range(q + 1):
                    shift = 1 << s
                    length -= shift
                    dst = win[s % 2]
                    if s:
                        pool.wait_ge(s_win, done)
                    pool.tensor_tensor(dst[:, :, 0:length], src[:, :, 0:length], src[:, :, shift:shift + length],
                                       ALU.add).then_inc(s_win, 1)
                    done += 1
                    src = dst

        @block.vector
        def _(dve):
            def low(m):
                if m >= TOTAL:
                    return
                dve.wait_ge(s_wh, m + 1)
                dve.tensor_tensor(w_lo[:, m % 2, 0:width(m)], raw[:, m % 2, 0:width(m)],
                                  w_hi[:, m % 2, 0:width(m)].bitcast(F32), ALU.subtract).then_inc(s_wl, 1)

            def pool_in(q):
                dve.wait_ge(s_win, (q + 1) * (q + 2) // 2)
                dve.wait_ge(m_ic, 16 * (q + 1))
                if q:
                    dve.wait_ge(s_pl, q)
                src, half = win[q % 2], WINDOWS[q] // 2
                parts = ((0, SEQS[0], PB), (SEQS[0], T, 3 * PB))
                for lo, hi, border in parts:
                    n = hi - lo
                    ins = dve.tensor_tensor(pooled[:, :, lo:hi], src[:, :, lo + border - half:lo + border - half + n],
                                            icnt[:, lo:hi].unsqueeze(1).to_broadcast([P, 2, n]), ALU.mult)
                ins.then_inc(s_cnt, 1)
                dve.wait_ge(s_cnt, q + 1)
                for lo, hi, border in parts:
                    ins = dve.tensor_tensor(pooled[:, :, lo:hi], pooled[:, :, lo:hi],
                                            up[:, :, lo + border:hi + border], ALU.subtract)
                ins.then_inc(s_pool, 1)

            def split_pooled(q):
                dve.wait_ge(s_ph, q + 1)
                if q:
                    dve.wait_ge(s_mm, 8 * (q - 1) + ORDER.index((MX, 1)) + 1)
                dve.tensor_tensor(pl_lo[:], pooled[:], pl_hi[:].bitcast(F32), ALU.subtract).then_inc(s_pl, 1)

            def split_result(q):
                dve.wait_ge(s_mh, q + 1)
                dve.tensor_tensor(m_lo[:, 2 * q:2 * q + 2, :], mx[:], m_hi[:, 2 * q:2 * q + 2, :].bitcast(F32),
                                  ALU.subtract).then_inc(s_ml, 1)

            dve.wait_ge(m_ps, 16)
            dve.tensor_scalar(pscale[:], pscale[:], 0.5, None, ALU.mult).then_inc(s_half, 1)
            low(0)
            low(1)
            for q in range(NQ):
                m = NUN * q
                low(m + 2)
                low(m + 3)
                if q:
                    split_result(q - 1)
                low(m + 4)
                pool_in(q)
                dve.wait_ge(s_ev, 8 * q + ORDER.index((GA, 1)) + 1)
                both = ya[:, 2 * q:2 * q + 2, :]
                dve.scalar_tensor_tensor(out=both, in0=tg[:], scalar=1.0, in1=both, op0=ALU.add, op1=ALU.mult)\
                   .then_inc(s_ga, 1)
                split_pooled(q)
                low(m + 5)
                low(m + 6)
                low(m + 7)
                dve.wait_ge(s_ev, 8 * q + ORDER.index((GB, 1)) + 1)
                dve.scalar_tensor_tensor(out=mx[:], in0=tg[:], scalar=1.0, in1=mx[:], op0=ALU.add, op1=ALU.mult)\
                   .then_inc(s_gb, 1)
                dve.wait_ge(s_gb, q + 1)
                dve.wait_ge(s_ga, q + 1)
                dve.scalar_tensor_tensor(out=mx[:], in0=both, scalar=0.5, in1=mx[:], op0=ALU.mult, op1=ALU.add)\
                   .then_inc(s_m, 1)
                low(m + 8)
            split_result(NQ - 1)


def residual(nc, A, cst, h_hi, h_lo, ya, m_hi, m_lo, h2, xa, prob):
    with ExitStack() as ctx:
        a = Alloc(nc, ctx)
        ident, tri_f, tri_b, ones, neg_half = cst
        wo_raw = a.sb("wo_raw", [P, KD, D])
        free_k = KD * T // D
        more_hi, more_lo = (a.sb(n, [P, KD - free_k, D], F32R) for n in ("wo_hi", "wo_lo"))
        room_hi, room_lo = (t[:].rearrange("p k t -> p (k t)") for t in (h_hi, h_lo))
        wo_hi, wo_lo = ([room[:, k * D:(k + 1) * D] for k in range(free_k)] + [more[:, k] for k in range(KD - free_k)]
                        for room, more in ((room_hi, more_hi), (room_lo, more_lo)))
        rows = ya[:].rearrange("p k t -> p (k t)")
        xin, x2, hh = (rows[:, i * 2 * D:(i + 1) * 2 * D].rearrange("p (s n) -> p s n", s=2) for i in range(3))
        hhT = a.sb("hhT", [P, 2, KD, P])
        sq = a.sb("sq2", [P, D])
        nffn = a.sb("nffn", [P, D])
        wr = a.sb("wr", [P, KD, E])
        ssq = a.sb("ssq2", [P, NT])
        rstd = a.sb("rstd2", [P, NT])
        mxl = a.sb("mxl", [P, NT])
        den = a.sb("den", [P, NT])
        p_o = [a.ps(f"p_o{i}", [P, 1024]) for i in range(2)]
        p_t = a.ps("p_t", [P, 1024])
        p_l = a.ps("p_l", [P, 512])
        m_c, s_woh, s_wol = a.sems("m_c", "r_woh", "r_wol")
        s_wo = a.sems(*[f"r_wo{k}" for k in range(KD)])
        s_x = a.sems("r_x0", "r_x1")
        s_xa = a.sems("r_xa0", "r_xa1")
        s_h2 = a.sems("r_h20", "r_h21")
        s_o, s_x2, s_sq, s_rs, s_h, s_t, s_ht, s_l, s_mx, s_e, s_den = a.sems(
            "r_o", "r_x2", "r_sq", "r_rs", "r_h", "r_t", "r_ht", "r_l", "r_mx", "r_e", "r_den")

        block = ctx.enter_context(nc.Block())

        @block.sync
        def _(sp):
            for k in range(KD):
                sp.dma_start(wo_raw[:, k], A["w_o"][k]).then_inc(s_wo[k], 16)
            for t in range(2):
                sp.dma_start(xin[:, t, :], A["x"][t]).then_inc(s_x[t], 16)
            sp.dma_start(nffn[:], A["norm_ffn"].partition_broadcast(P)).then_inc(m_c, 16)
            sp.dma_start(wr[:], A["w_router"]).then_inc(m_c, 16)
            for t in range(NT):
                sp.wait_ge(s_x2, t + 1)
                sp.dma_start(xa[t * P:(t + 1) * P, :], x2[:, t % 2, :]).then_inc(s_xa[t % 2], 16)
                if t + 2 < NT:
                    sp.dma_start(xin[:, t % 2, :], A["x"][t + 2]).then_inc(s_x[t % 2], 16)
                sp.wait_ge(s_h, t + 1)
                sp.dma_start(h2[t * P:(t + 1) * P, :], hh[:, t % 2, :]).then_inc(s_h2[t % 2], 16)
            for s in s_xa + s_h2:
                sp.wait_ge(s, 16 * NT // 2)

        @block.tensor
        def _(pe):
            def route(t):
                pe.wait_ge(s_h, t + 1)
                if t:
                    pe.wait_ge(s_ht, t)
                for k in range(KD):
                    mm = pe.transpose(p_t[:, k * P:(k + 1) * P], hh[:, t % 2, k * P:(k + 1) * P], ident[:])
                mm.then_inc(s_t, 1)

            def logits(t):
                pe.wait_ge(m_c, 32)
                pe.wait_ge(s_ht, t + 1)
                for k in range(KD):
                    mm = pe.matmul(p_l[:, t * E:(t + 1) * E], hhT[:, t % 2, k, :], wr[:, k, :],
                                   start=(k == 0), stop=(k == KD - 1))
                mm.then_inc(s_l, 1)

            for t in range(NT):
                if t >= 2:
                    pe.wait_ge(s_x2, t - 1)
                for k in range(KD):
                    pe.wait_ge(s_wol, k + 1)
                    for n in range(2):
                        cols = slice(n * 512, (n + 1) * 512)
                        for i, (m, w) in enumerate(three(m_hi, m_lo, wo_hi, wo_lo)):
                            mm = pe.matmul(p_o[t % 2][:, cols], m[:, k, t * P:(t + 1) * P], w[k][:, cols],
                                           start=(k == 0 and i == 0), stop=(k == KD - 1 and i == 2))
                mm.then_inc(s_o, 1)
                if t:
                    route(t - 1)
                if t > 1:
                    logits(t - 2)
            route(NT - 1)
            logits(NT - 2)
            logits(NT - 1)

        @block.scalar
        def _(act):
            def softmax_exp(t):
                act.activation(prob[:, t, :], p_l[:, t * E:(t + 1) * E], ACT.Exp, bias=mxl[:, t:t + 1],
                               accum_out=den[:, t:t + 1]).then_inc(s_e, 1)

            for k in range(KD):
                act.wait_ge(s_wo[k], 16)
                act.activation(wo_hi[k], wo_raw[:, k], ACT.Copy).then_inc(s_woh, 1)
            for t in range(NT):
                act.wait_ge(s_x2, t + 1)
                if t:
                    act.wait_ge(s_sq, t)
                act.activation(sq[:], x2[:, t % 2, :], ACT.Square, accum_out=ssq[:, t:t + 1]).then_inc(s_sq, 1)
                if t:
                    act.wait_ge(s_t, t)
                    if t > 2:
                        act.wait_ge(s_l, t - 2)
                    act.activation(hhT[:, (t - 1) % 2].rearrange("p k n -> p (k n)"), p_t[:], ACT.Copy)\
                       .then_inc(s_ht, 1)
            act.wait_ge(s_t, NT)
            act.wait_ge(s_l, NT - 2)
            act.activation(hhT[:, (NT - 1) % 2].rearrange("p k n -> p (k n)"), p_t[:], ACT.Copy).then_inc(s_ht, 1)
            act.wait_ge(s_mx, NT)
            for t in range(NT):
                softmax_exp(t)

        @block.gpsimd
        def _(pool):
            for t in range(NT):
                pool.wait_ge(s_sq, t + 1)
                rs = Steps(pool, s_rs, 2 * t)
                rs(pool.tensor_scalar(ssq[:, t:t + 1], ssq[:, t:t + 1], 1.0 / D, EPS, ALU.mult, ALU.add))
                rs(pool.tensor_tensor(rstd[:, t:t + 1], ssq[:, t:t + 1], neg_half[:, 0:1], ALU.pow))

        @block.vector
        def _(dve):
            def norm(t):
                dve.wait_ge(s_rs, 2 * t + 2)
                if t >= 2:
                    dve.wait_ge(s_t, t - 1)
                    dve.wait_ge(s_h2[t % 2], 16 * (t // 2))
                dve.scalar_tensor_tensor(out=hh[:, t % 2, :], in0=x2[:, t % 2, :], scalar=rstd[:, t:t + 1],
                                         in1=nffn[:], op0=ALU.mult, op1=ALU.mult).then_inc(s_h, 1)

            for k in range(KD):
                dve.wait_ge(s_woh, k + 1)
                dve.tensor_tensor(wo_lo[k], wo_raw[:, k], wo_hi[k].bitcast(F32), ALU.subtract)\
                   .then_inc(s_wol, 1)
            dve.wait_ge(m_c, 32)
            for t in range(NT):
                dve.wait_ge(s_x[t % 2], 16 * (t // 2 + 1))
                dve.wait_ge(s_o, t + 1)
                if t >= 2:
                    dve.wait_ge(s_xa[t % 2], 16 * (t // 2))
                    dve.wait_ge(s_sq, t - 1)
                    dve.wait_ge(s_h, t - 1)
                dve.tensor_tensor(x2[:, t % 2, :], p_o[t % 2][:], xin[:, t % 2, :], ALU.add).then_inc(s_x2, 1)
                norm(t)
            dve.wait_ge(s_l, NT)
            for t in range(NT):
                dve.tensor_reduce(mxl[:, t:t + 1], p_l[:, t * E:(t + 1) * E], AX_X, ALU.max, negate=True)\
                   .then_inc(s_mx, 1)
            dve.wait_ge(s_e, NT)
            dve.reciprocal(den[:], den[:]).then_inc(s_den, 1)
            dve.wait_ge(s_den, 1)
            dve.tensor_tensor(prob[:], prob[:], den[:].unsqueeze(2).to_broadcast([P, NT, E]), ALU.mult)


def load_unit(sp, A, raw, s_raw, e, u):
    w = UNITS[u] * P * 3 * KD
    at = sum(UNITS[:u]) * P * 3 * KD * P
    src = A["w_e"][bass.ds(e, 1), at:at + w * P].rearrange("e (p n) -> p (e n)", p=P)
    sp.dma_start(raw[:, u % RAW, 0:w], src).then_inc(s_raw[u % RAW], 16)


def choose(nc, A, cst, prob, raw, s_raw, idx, aff):
    with ExitStack() as ctx:
        a = Alloc(nc, ctx)
        ident = cst[0]
        ROWS = 32 + E
        pblk = a.sb("pblk", [P, NTP, ROWS])
        pt = a.sb("pt", [ROWS, SEQS[0]])
        work = a.sb("work", [ROWS, SEQS[0]])
        tops = a.sb("tops", [ROWS, CAPS[0] // 8, 8])
        thr, cap, above = (a.sb(n, [ROWS, 1]) for n in ("thr", "cap", "above"))
        gt, eq, rank, one = (a.sb(n, [ROWS, SEQS[0]]) for n in ("gt", "eq", "rank", "one"))
        posT = a.sb("posT", [P, NTP, ROWS])
        slot1 = a.sb("slot1", [P, CAPS[0]])
        tokid = a.sb("tokid", [P, NT])
        oh_p = a.sb("oh_p", [P, NTP, E, CAPS[0]])
        oh_s = a.sb("oh_s", [P, NT - NTP, E, CAPS[1]])
        pairs = a.sb("pairs", [P, NT, E, 2])
        p_s = a.ps("c_ps", [P, 512])
        p_t = a.ps("c_pt_", [P, 512])
        p_l = a.ps("c_pl", [P, 512])
        m_c, s_c, s_pb, s_pt, s_ch, s_pos, s_posT, s_oh, s_ia, s_init = a.sems(
            "c_m", "c_c", "c_pb", "c_pt", "c_ch", "c_pos", "c_posT", "c_oh", "c_ia", "c_init")

        block = ctx.enter_context(nc.Block())

        @block.sync
        def _(sp):
            sp.dma_start(slot1[:], A["slot1"].partition_broadcast(P)).then_inc(m_c, 16)
            sp.dma_start(tokid[:], A["tokid"]).then_inc(m_c, 16)
            for u in range(RAW):
                load_unit(sp, A, raw, s_raw, 0, u)

        @block.tensor
        def _(pe):
            pe.wait_ge(s_pb, 1)
            for b in range(NTP):
                mm = pe.transpose(p_s[0:ROWS, b * P:(b + 1) * P], pblk[:, b, :], ident[:])
            mm.then_inc(s_pt, 1)
            pe.wait_ge(s_pos, 1)
            for b in range(NTP):
                mm = pe.transpose(p_t[:, b * ROWS:(b + 1) * ROWS], rank[:, b * P:(b + 1) * P], ident[0:ROWS, 0:ROWS])
            mm.then_inc(s_posT, 1)
            pe.wait_ge(s_oh, 1)
            for e in range(E):
                for b in range(NTP):
                    pe.matmul(p_l[0:CAPS[0], 2 * e:2 * e + 2], oh_p[:, b, e, :], pairs[:, b, e, :],
                              start=(b == 0), stop=(b == NTP - 1))
                for b in range(NT - NTP):
                    mm = pe.matmul(p_l[CAPS[0]:SLOTS, 2 * e:2 * e + 2], oh_s[:, b, e, :], pairs[:, NTP + b, e, :],
                                   start=(b == 0), stop=(b == NT - NTP - 1))
            mm.then_inc(s_ia, 1)

        @block.gpsimd
        def _(pool):
            pool.memset(one[:], 1.0)
            pool.memset(pblk[:], -1.0)
            pool.memset(thr[:], 0.0)
            pool.memset(cap[:], float(CAPS[1])).then_inc(s_init, 1)
            pool.wait_ge(s_init, 1)
            pool.memset(cap[0:32], float(CAPS[0])).then_inc(s_init, 1)

        @block.vector
        def _(dve):
            ch = Steps(dve, s_ch)
            dve.wait_ge(m_c, 32)
            dve.wait_ge(s_init, 2)
            dve.tensor_copy(pblk[:, :, 0:E], prob[:, 0:NTP, :])
            dve.tensor_copy(pblk[:, 0:NT - NTP, 32:ROWS], prob[:, NTP:NT, :]).then_inc(s_pb, 1)
            dve.tensor_copy(pairs[:, :, :, 0], tokid[:].unsqueeze(2).to_broadcast([P, NT, E]))
            dve.tensor_copy(pairs[:, :, :, 1], prob[:])
            dve.wait_ge(s_pt, 1)
            ch(dve.tensor_copy(pt[:], p_s[0:ROWS, :]))
            ch(dve.tensor_copy(work[:], pt[:]))
            for r in range(CAPS[0] // 8):
                ch(dve.max(tops[:, r, :], work[:]))
                if r < CAPS[0] // 8 - 1:
                    ch(dve.match_replace(work[:], tops[:, r, :], work[:], -2.0))
            dve.tensor_copy(thr[0:E, :], tops[0:E, CAPS[0] // 8 - 1, 7:8])
            ch(dve.tensor_copy(thr[32:ROWS, :], tops[32:ROWS, CAPS[1] // 8 - 1, 7:8]))
            ch(dve.tensor_scalar(gt[:], pt[:], thr[:], 0.0, ALU.is_gt, ALU.add, accum_out=above[:]))
            ch(dve.tensor_scalar(eq[:], pt[:], thr[:], None, ALU.is_equal))
            ch(dve.tensor_tensor_scan(rank[:], one[:], eq[:], 0.0, ALU.mult, ALU.add))
            ch(dve.tensor_tensor(above[:], cap[:], above[:], ALU.subtract))
            ch(dve.scalar_tensor_tensor(out=eq[:], in0=rank[:], scalar=above[:], in1=eq[:],
                                        op0=ALU.is_le, op1=ALU.mult))
            ch(dve.tensor_tensor(gt[:], gt[:], eq[:], ALU.add))
            ch(dve.tensor_tensor_scan(work[:], one[:], gt[:], 0.0, ALU.mult, ALU.add))
            dve.tensor_tensor(rank[:], work[:], gt[:], ALU.mult).then_inc(s_pos, 1)
            dve.wait_ge(s_posT, 1)
            ch(dve.tensor_copy(posT[:].rearrange("p b r -> p (b r)"), p_t[:, 0:NTP * ROWS]))
            for b in range(NTP):
                dve.tensor_tensor(oh_p[:, b], posT[:, b, 0:E].unsqueeze(2).to_broadcast([P, E, CAPS[0]]),
                                  slot1[:].unsqueeze(1).to_broadcast([P, E, CAPS[0]]), ALU.is_equal)
            for b in range(NT - NTP):
                ins = dve.tensor_tensor(oh_s[:, b], posT[:, b, 32:ROWS].unsqueeze(2).to_broadcast([P, E, CAPS[1]]),
                                        slot1[:, 0:CAPS[1]].unsqueeze(1).to_broadcast([P, E, CAPS[1]]), ALU.is_equal)
            ins.then_inc(s_oh, 1)
            dve.wait_ge(s_ia, 1)
            got = p_l[0:SLOTS, 0:2 * E].rearrange("p (e k) -> p e k", k=2)
            dve.tensor_copy(idx[:, 0:E], got[:, :, 0])
            dve.tensor_copy(idx[:, E:E + 1], got[:, 0:1, 0])
            dve.tensor_copy(aff[:], got[:, :, 1]).then_inc(s_c, 1)
            dve.wait_ge(s_c, 1)


def experts(nc, A, cst, raw, s_raw, h2, xa, idx, aff):
    with ExitStack() as ctx:
        a = Alloc(nc, ctx)
        ident = cst[0]
        wh = a.sb("wh", [P, 2, UW], F32R)
        wl = a.sb("wl", [P, 2, UW], F32R)
        idx_g = a.sb("idx_g", [SLOTS, 1], I32)
        idx_s = a.sb("idx_s", [SLOTS, 1], I32)
        aff_c = a.sb("aff_c", [SLOTS, 1])
        xe = a.sb("xe", [SLOTS, D])
        xh = a.sb("xh", [P, KD * SLOTS], F32R)
        xl = a.sb("xl", [P, KD * SLOTS], F32R)
        tg = a.sb("tg", [SLOTS, 2, UT * P])
        hid = a.sb("hid", [SLOTS, 2, UT * P])
        hh = a.sb("hid_hi", [P, 2, UT * SLOTS], F32R)
        hl = a.sb("hid_lo", [P, 2, UT * SLOTS], F32R)
        ye = a.sb("ye", [SLOTS, D])
        p_gu = [a.ps(f"p_gu{i}", [P, 512]) for i in range(2)]
        p_h = [a.ps(f"p_h{i}", [P, 512]) for i in range(2)]
        p_x = a.ps("p_x", [P, 1024])
        p_y = a.ps("p_y", [P, 1024])
        s_wh, s_wl, s_gu, s_dn, s_hid, s_t, s_hl, s_xl, s_ye, s_free = a.sems(
            "e_wh", "e_wl", "e_gu", "e_dn", "e_hid", "e_t", "e_hl", "e_xl", "e_ye", "e_free")
        s_tg, s_sg, s_hh, s_ig, s_is, s_g, s_xt, s_xh, s_sc, s_aff = a.sems(
            "e_tg", "e_sg", "e_hh", "e_ig", "e_is", "e_g", "e_xt", "e_xh", "e_sc", "e_aff")
        s_go = a.sem("e_go")
        W0 = 3 * RAW

        DOWN = UT * P * 2 * KD

        def pieces(nt):
            gu, dn = nt * P * 2 * KD, nt * P * KD
            return ((0, gu // 2, 0), (gu // 2, gu, gu // 2), (gu, gu + dn, DOWN))

        def tiles(ap):
            return ap.rearrange("p (k s) -> p k s", k=KD)

        turned = p_x[:].rearrange("p (k s) -> p k s", k=KD)[:, :, 0:SLOTS]

        def following(e, u):
            return (e + 1, 0) if u == NU - 1 else (e, u + 1)

        block = ctx.enter_context(nc.Block())

        @block.sync
        def _(sp):
            def load(e, u):
                n = NU * e + u
                sp.wait_ge(s_wh, 3 * n + 3)
                sp.wait_ge(s_wl, 3 * n + 3)
                load_unit(sp, A, raw, s_raw, e, u)

            for u in range(RAW, NU):
                load(0, u)
            with sp.Fori(1, E) as e:
                for u in range(NU):
                    load(e, u)

        @block.gpsimd
        def _(pool):
            def gather(e):
                pool.tensor_copy(idx_g[:], idx[:, bass.ds(e, 1)]).then_inc(s_ig, 1)
                pool.wait_ge(s_ig, e + 1)
                pool.sem_inc(s_go, 1)
                pool.indirect_dma_start(xe[:], None, h2, bass.IndirectOffsetOnAxis(ap=idx_g[:, 0:1], axis=0))\
                    .then_inc(s_g, 16)

            pool.sem_inc(s_free, 1)
            gather(0)
            with pool.Fori(0, E) as e:
                pool.wait_ge(s_xt, e + 1)
                gather(e + 1)
                pool.tensor_copy(idx_s[:], idx[:, bass.ds(e, 1)]).then_inc(s_is, 1)
                pool.wait_ge(s_is, e + 1)
                pool.wait_ge(s_ye, e + 2)
                pool.sem_inc(s_go, 1)
                pool.indirect_dma_start(xa, bass.IndirectOffsetOnAxis(ap=idx_s[:, 0:1], axis=0), ye[:], None,
                                        compute_op=ALU.add).then_inc(s_sc, 16)
                pool.wait_ge(s_sc, 16 * e + 16)
                pool.sem_inc(s_free, 1)
            pool.wait_ge(s_g, 16 * (E + 1))

        @block.scalar
        def _(act):
            def high(e, u, k):
                n = NU * e + u
                if k == 0:
                    act.wait_ge(s_raw[u % RAW], (16 * NU // RAW) * e + 16 * (u // RAW + 1))
                    act.wait_ge(s_gu, n + 1)
                if k == 2:
                    act.wait_ge(s_dn, n + 1)
                lo, hi, at = pieces(UNITS[u])[k]
                act.activation(wh[:, u % 2, at:at + hi - lo], raw[:, u % RAW, lo:hi], ACT.Copy).then_inc(s_wh, 1)

            def tokens(e):
                act.wait_ge(s_xt, e + 1)
                act.wait_ge(s_gu, NU * e + 2)
                act.activation(tiles(xh[:]), turned, ACT.Copy).then_inc(s_xh, 1)

            def expert(e, last):
                for u, nt in enumerate(UNITS):
                    n = NU * e + u
                    ahead = None if last and u == NU - 1 else following(e, u)
                    if ahead:
                        high(*ahead, 0)
                        high(*ahead, 1)
                    act.wait_ge(s_gu, n + 3)
                    act.wait_ge(s_hid, n + 1)
                    act.activation(tg[:, u % 2, 0:nt * P], p_gu[u % 2][0:SLOTS, 0:nt * P], ACT.Tanh, scale=0.5)\
                       .then_inc(s_tg, 1)
                    if ahead:
                        high(*ahead, 2)
                    if u == NU - 1:
                        tokens(e + 1)
                    act.wait_ge(s_t, n + 3)
                    act.wait_ge(s_dn, n + 1)
                    act.activation(hh[:, u % 2, 0:nt * SLOTS], p_h[u % 2][:, 0:nt * SLOTS], ACT.Copy)\
                       .then_inc(s_hh, 1)

            act.sem_inc(s_wh, W0)
            tokens(0)
            for k in range(3):
                high(0, 0, k)
            with act.Fori(0, E - 1) as e:
                expert(e, False)
            expert(E - 1, True)

        @block.vector
        def _(dve):
            def low(e, u, k):
                lo, hi, at = pieces(UNITS[u])[k]
                to = slice(at, at + hi - lo)
                dve.wait_ge(s_wh, 3 * (NU * e + u) + (W0 + k + 1))
                dve.tensor_tensor(wl[:, u % 2, to], raw[:, u % RAW, lo:hi], wh[:, u % 2, to].bitcast(F32),
                                  ALU.subtract).then_inc(s_wl, 1)

            def tokens(e):
                dve.wait_ge(s_xh, e + 1)
                dve.tensor_tensor(tiles(xl[:]), turned, tiles(xh[:].bitcast(F32)), ALU.subtract).then_inc(s_xl, 1)

            def expert(e, last):
                dve.wait_ge(s_ye, e + 1)
                dve.tensor_copy(aff_c[:], aff[:, bass.ds(e, 1)]).then_inc(s_aff, 1)
                for u, nt in enumerate(UNITS):
                    n = NU * e + u
                    w = nt * P
                    ahead = None if last and u == NU - 1 else following(e, u)
                    if ahead:
                        low(*ahead, 0)
                        low(*ahead, 1)
                    dve.wait_ge(s_tg, n + 1)
                    dve.scalar_tensor_tensor(out=tg[:, u % 2, 0:w], in0=tg[:, u % 2, 0:w], scalar=1.0,
                                             in1=p_gu[u % 2][0:SLOTS, 0:w], op0=ALU.add, op1=ALU.mult)\
                       .then_inc(s_sg, 1)
                    dve.wait_ge(s_sg, n + 1)
                    dve.wait_ge(s_t, n + 1)
                    dve.scalar_tensor_tensor(out=hid[:, u % 2, 0:w], in0=tg[:, u % 2, 0:w], scalar=0.5,
                                             in1=p_gu[u % 2][0:SLOTS, w:2 * w], op0=ALU.mult, op1=ALU.mult)\
                       .then_inc(s_hid, 1)
                    if ahead:
                        low(*ahead, 2)
                    if u == NU - 1:
                        tokens(e + 1)
                    dve.wait_ge(s_hh, n + 1)
                    dve.tensor_tensor(hl[:, u % 2, 0:nt * SLOTS], p_h[u % 2][:, 0:nt * SLOTS],
                                      hh[:, u % 2, 0:nt * SLOTS].bitcast(F32), ALU.subtract).then_inc(s_hl, 1)
                dve.wait_ge(s_aff, e + 1)
                dve.wait_ge(s_dn, NU * e + (NU + 2))
                dve.wait_ge(s_free, e + 1)
                dve.tensor_scalar(ye[:], p_y[0:SLOTS, :], aff_c[:], None, ALU.mult).then_inc(s_ye, 1)

            dve.sem_inc(s_wl, W0)
            dve.sem_inc(s_hid, 2)
            dve.sem_inc(s_hl, 2)
            dve.sem_inc(s_xl, 1)
            dve.sem_inc(s_ye, 1)
            tokens(0)
            for k in range(3):
                low(0, 0, k)
            with dve.Fori(0, E - 1) as e:
                expert(e, False)
            expert(E - 1, True)

        @block.tensor
        def _(pe):
            def gate_up(e, u, half):
                n = NU * e + u
                pe.wait_ge(s_wl, 3 * n + (W0 + half + 1))
                if half == 0:
                    pe.wait_ge(s_hid, n + 1)
                w = 2 * UNITS[u] * P
                for k in range(half * KD // 2, (half + 1) * KD // 2):
                    for i, (xx, ww) in enumerate(((xh, wh), (xl, wh), (xh, wl))):
                        mm = pe.matmul(p_gu[u % 2][0:SLOTS, 0:w], xx[:, k * SLOTS:(k + 1) * SLOTS],
                                       ww[:, u % 2, k * w:(k + 1) * w],
                                       start=(k == 0 and i == 0), stop=(k == KD - 1 and i == 2))
                if half == 1:
                    mm.then_inc(s_gu, 1)

            def turn(e, u):
                n = NU * e + u
                pe.wait_ge(s_hid, n + 3)
                pe.wait_ge(s_hl, n + 1)
                for i in range(UNITS[u]):
                    mm = pe.transpose(p_h[u % 2][:, i * SLOTS:(i + 1) * SLOTS], hid[:, u % 2, i * P:(i + 1) * P],
                                      ident[0:SLOTS, 0:SLOTS])
                mm.then_inc(s_t, 1)

            def down(e, u):
                n = NU * e + u
                nt = UNITS[u]
                if u == 0:
                    pe.wait_ge(s_ye, e + 1)
                pe.wait_ge(s_hl, n + 3)
                pe.wait_ge(s_wl, 3 * n + (W0 + 3))
                for i in range(nt):
                    for half in range(2):
                        for j, (hx, ww) in enumerate(((hh, wh), (hl, wh), (hh, wl))):
                            c0 = DOWN + i * D + half * 512
                            mm = pe.matmul(p_y[0:SLOTS, half * 512:(half + 1) * 512],
                                           hx[:, u % 2, i * SLOTS:(i + 1) * SLOTS], ww[:, u % 2, c0:c0 + 512],
                                           start=(u == 0 and i == 0 and j == 0),
                                           stop=(u == NU - 1 and i == nt - 1 and j == 2))
                mm.then_inc(s_dn, 1)

            pe.sem_inc(s_gu, 2)
            pe.sem_inc(s_dn, 2)
            pe.sem_inc(s_t, 2)
            def tokens(e):
                pe.wait_ge(s_g, 16 * e + 16)
                pe.wait_ge(s_xl, e + 1)
                for k in range(KD):
                    mm = pe.transpose(turned[:, k, :], xe[:, k * P:(k + 1) * P],
                                      ident[0:SLOTS, 0:SLOTS])
                mm.then_inc(s_xt, 1)

            tokens(0)
            with pe.Fori(0, E) as e:
                pe.wait_ge(s_xl, e + 2)
                for u in range(NU):
                    gate_up(e, u, 0)
                    if u:
                        turn(e, u - 1)
                    gate_up(e, u, 1)
                    if u:
                        down(e, u - 1)
                tokens(e + 1)
                turn(e, NU - 1)
                down(e, NU - 1)


def final(nc, A, cst, xa, outs):
    with ExitStack() as ctx:
        a = Alloc(nc, ctx)
        neg_half = cst[4]
        x = a.sb("xf", [P, NT, D])
        o = a.sb("of", [P, NT, D])
        sq = a.sb("sqf", [P, D])
        nfin = a.sb("nfin", [P, D])
        ssq = a.sb("ssqf", [P, NT])
        rstd = a.sb("rstdf", [P, NT])
        s_x = a.sems(*[f"f_x{t}" for t in range(NT)])
        s_n, s_sq, s_rs, s_o, s_out = a.sems("f_n", "f_sq", "f_rs", "f_o", "f_out")
        block = ctx.enter_context(nc.Block())

        @block.sync
        def _(sp):
            for t in range(NT):
                sp.dma_start(x[:, t, :], xa[t * P:(t + 1) * P, :]).then_inc(s_x[t], 16)
            sp.dma_start(nfin[:], A["norm_final"].partition_broadcast(P)).then_inc(s_n, 16)
            for t in range(NT):
                out, row = (outs[0], t * P) if t < NTP else (outs[1], (t - NTP) * P)
                sp.wait_ge(s_o, t + 1)
                sp.dma_start(out[0, row:row + P, :], o[:, t, :]).then_inc(s_out, 16)
            sp.wait_ge(s_out, 16 * NT)

        @block.scalar
        def _(act):
            for t in range(NT):
                act.wait_ge(s_x[t], 16)
                if t:
                    act.wait_ge(s_sq, t)
                act.activation(sq[:], x[:, t, :], ACT.Square, accum_out=ssq[:, t:t + 1]).then_inc(s_sq, 1)

        @block.gpsimd
        def _(pool):
            for t in range(NT):
                pool.wait_ge(s_sq, t + 1)
                rs = Steps(pool, s_rs, 2 * t)
                rs(pool.tensor_scalar(ssq[:, t:t + 1], ssq[:, t:t + 1], 1.0 / D, EPS, ALU.mult, ALU.add))
                rs(pool.tensor_tensor(rstd[:, t:t + 1], ssq[:, t:t + 1], neg_half[:, 0:1], ALU.pow))

        @block.vector
        def _(dve):
            dve.wait_ge(s_n, 16)
            for t in range(NT):
                dve.wait_ge(s_x[t], 16)
                dve.wait_ge(s_rs, 2 * t + 2)
                dve.scalar_tensor_tensor(out=o[:, t, :], in0=x[:, t, :], scalar=rstd[:, t:t + 1], in1=nfin[:],
                                         op0=ALU.mult, op1=ALU.mult).then_inc(s_o, 1)


def build(nc, A, outs):
    acs = nc.dram_tensor("acs", (G * 2 * H, T), F32).ap()
    ys = nc.dram_tensor("ys", (G, P, 2, T), F32).ap()
    h2 = nc.dram_tensor("h2", (T, D), F32).ap()
    xa = nc.dram_tensor("xa", (T, D), F32).ap()
    with ExitStack() as ctx:
        a = Alloc(nc, ctx)
        cst = [a.sb(n, [P, P]) for n in ("ident", "tri_f", "tri_b", "ones")] + [a.sb("neg_half", [P, NT])]
        idx = a.sb("idx", [SLOTS, E + 1], I32)
        aff = a.sb("aff", [SLOTS, E])
        prob = a.sb("prob", [P, NT, E])
        with ExitStack() as front:
            f = Alloc(nc, front)
            h_hi, h_lo = (f.sb(n, [P, KD, T], F32R) for n in ("h_hi", "h_lo"))
            with ExitStack() as ssd:
                head_tab = Alloc(nc, ssd).sb("head_tab", [P, G, 5, NT, 2 * H])
                prepare(nc, A, cst, h_hi, h_lo, head_tab, acs)
                mixer(nc, A, cst, h_hi, h_lo, head_tab, acs, ys)
            ya = f.sb("ya", [P, KD, T])
            ssm_out(nc, A, ys, ya)
            m_hi, m_lo = (f.sb(n, [P, KD, T], F32R) for n in ("m_hi", "m_lo"))
            gates(nc, A, h_hi, h_lo, ya, m_hi, m_lo)
            residual(nc, A, cst, h_hi, h_lo, ya, m_hi, m_lo, h2, xa, prob)
        with ExitStack() as late:
            l = Alloc(nc, late)
            raw = l.sb("raw", [P, RAW, UW])
            s_raw = l.sems(*[f"e_raw{i}" for i in range(RAW)])
            choose(nc, A, cst, prob, raw, s_raw, idx, aff)
            experts(nc, A, cst, raw, s_raw, h2, xa, idx, aff)
        final(nc, A, cst, xa, outs)


def kernel(**inputs):
    import numpy as np
    import concourse.bacc as _bacc
    from concourse import mybir as _mybir
    from concourse.bass_utils import run_bass_kernel_spmd as _run

    w = {k: np.asarray(v) for k, v in inputs.items()}
    x = np.concatenate([w["x_prompt"][0], w["x_sample"][0]])
    w_in = w["w_in"][0].reshape(KD, P, -1).transpose(1, 0, 2)
    di = G * GW
    o_x, o_B, o_C = di, 2 * di, 2 * di + G * P
    o_dt = o_C + G * P
    o_u, o_ga, o_gb = o_dt + NH, o_dt + NH + D, o_dt + NH + 2 * D
    z = w_in[:, :, :di].reshape(P, KD, G, GW)
    xs = w_in[:, :, o_x:o_B].reshape(P, KD, G, 2, P)
    b = w_in[:, :, o_B:o_C].reshape(P, KD, G, 1, P)
    c = w_in[:, :, o_C:o_dt].reshape(P, KD, G, 1, P)
    dtw = w_in[:, :, o_dt:o_u].reshape(P, KD, 2, G, H)
    pool_in = [w_in[:, :, o:o + D].reshape(P, KD, NQ, 2, P) for o in (o_u, o_ga, o_gb)]

    def by_head(f, bk):
        return np.stack([f, bk]).reshape(2, G, H).transpose(1, 0, 2).reshape(NH)

    taps = np.concatenate([w["conv_w"][0], w["conv_b"]])

    def tiles(a, off, n):
        return a[:, off:off + G * n * P].reshape(-1, G, n, P)
    cx, cb, cc = tiles(taps, 0, 2), tiles(taps, di, 1), tiles(taps, di + G * P, 1)
    conv_tab = np.concatenate([cx, cb, cc], axis=2).transpose(3, 1, 2, 0).reshape(P, G, -1)
    nw = w["ssm_norm_w"][0].reshape(G, 2, P).transpose(2, 0, 1)
    skip = np.broadcast_to(w["d_skip"][0].reshape(1, G, H), (P, G, H))
    gate = w["w_gate"][0].reshape(E, KD, P, FT, P)
    up = w["w_up"][0].reshape(E, KD, P, FT, P)
    down = w["w_down"][0].reshape(E, FT, P, D)
    w_e = np.empty((E, P * FT * P * 3 * KD), np.float32)
    t0 = at = 0
    for nt in UNITS:
        gu = np.stack([gate[:, :, :, t0:t0 + nt], up[:, :, :, t0:t0 + nt]], axis=3)
        gu = gu.transpose(0, 2, 1, 3, 4, 5).reshape(E, P, -1)
        dn = down[:, t0:t0 + nt].transpose(0, 2, 1, 3).reshape(E, P, -1)
        unit = np.concatenate([gu, dn], axis=2).reshape(E, -1)
        w_e[:, at:at + unit.shape[1]] = unit
        at += unit.shape[1]
        t0 += nt
    tri = np.tri(P, dtype=np.float32)
    counts = []
    for win in WINDOWS:
        for s in SEQS:
            pos = np.arange(s)
            n = np.clip(pos + win - win // 2, 0, s) - np.clip(pos - win // 2, 0, s)
            counts.append(1.0 / n)
    arrays = {
        "x": x.reshape(NT, P, D),
        "xT": x.T.reshape(KD, P, T).transpose(1, 0, 2),
        "norm_mix": w["norm_mix_w"][0].reshape(KD, P).T,
        "w_dt": dtw.transpose(0, 1, 3, 2, 4).reshape(P, KD, NH),
        "dt_bias": by_head(w["dt_bias_f"][0], w["dt_bias_b"][0]),
        "a_log": by_head(w["a_log_f"][0], w["a_log_b"][0]),
        "w_x": np.concatenate([np.concatenate([xs, b, c], axis=3).transpose(2, 3, 0, 1, 4).reshape(G, 4, P, -1),
                               z.reshape(P, 2, KD // 2, G, GW).transpose(3, 1, 0, 2, 4).reshape(G, 2, P, -1)],
                              axis=1),
        "conv_tab": conv_tab,
        "d_skip": skip,
        "ssm_norm": nw.reshape(P, 2 * G),
        "w_g": np.concatenate(pool_in, axis=3).transpose(2, 3, 0, 1, 4).reshape(NQ, 6, P, -1),
        "w_s": w["w_ssm_out"][0].reshape(2, KD, P, KD, P).transpose(3, 0, 2, 1, 4).reshape(2 * KD, P, -1),
        "w_p": w["w_pool"][0].reshape(NQ, 2, P, 2 * P).transpose(0, 2, 1, 3).reshape(NQ, P, -1),
        "pool_scale": w["pool_scale"][0].reshape(KD, P).T,
        "w_o": w["w_o"][0].reshape(KD, P, D),
        "norm_ffn": w["norm_ffn_w"][0],
        "w_router": w["w_router"][0].reshape(KD, P, E).transpose(1, 0, 2),
        "w_e": w_e,
        "norm_final": w["norm_final_w"],
        "ident": np.eye(P, dtype=np.float32),
        "tri_f": tri.T,
        "tri_b": tri,
        "icnt": np.concatenate(counts).reshape(NQ, T).astype(np.float32),
        "slot1": np.arange(1, CAPS[0] + 1, dtype=np.float32),
        "tokid": np.arange(T, dtype=np.float32).reshape(NT, P).T,
    }
    nc = _bacc.Bacc("TRN2", target_bir_lowering=False, num_devices=1)
    arrays = {f"in_{k}": np.ascontiguousarray(v) for k, v in arrays.items()}
    A = {k[3:]: nc.dram_tensor(k, v.shape, _mybir.dt.from_np(v.dtype), kind="ExternalInput").ap()
         for k, v in arrays.items()}
    outs = [nc.dram_tensor(f"out_{i}", (1, s, D), F32, kind="ExternalOutput").ap() for i, s in enumerate(SEQS)]
    build(nc, A, outs)
    r = _run(nc, [arrays], core_ids=[0])
    return tuple(r.results[0][f"out_{i}"] for i in range(len(SEQS)))
```
